# Optimizing a Trainium2 kernel written in Bass

```python
import math, functools
import jax, jax.numpy as jnp
from jax import lax
import numpy as np

D_MODEL = 2048
BATCH = 1
SEQ = 512
DEPTH = 1
DEC_BATCH = 8
DEC_SEQ = 4
PAST_LEN = 2048
PAGE_SIZE = 128

MIX_WIDTH = D_MODEL
NSA_HEAD_DIM = 64
NSA_HEADS = (3 * MIX_WIDTH // 4) // NSA_HEAD_DIM
NSA_KV_HEADS = 4
NSA_GROUP = NSA_HEADS // NSA_KV_HEADS
CMP_STRIDE = 16
CMP_LEN = 2 * CMP_STRIDE
SEL_LEN = 64
SEL_TOP_N = 16
NSA_WINDOW = 512
DIL_HEAD_DIM = 128
DIL_CONFIGS = ((128, 1), (512, 4), (2048, 16))
DIL_GROUPS = len(DIL_CONFIGS)
DIL_HEADS = (MIX_WIDTH // 4) // DIL_HEAD_DIM
N_ATT_HEADS = NSA_HEADS + DIL_GROUPS * DIL_HEADS
NUM_BUCKETS = 32
MAX_DISTANCE = 128
N_EXPERT_GROUPS = 4
EXPERTS_PER_GROUP = 4
N_EXPERTS = N_EXPERT_GROUPS * EXPERTS_PER_GROUP
TOP_K_EXPERT = 2
D_EXPERT = D_MODEL // 8
Q_BLOCK = 128
ALPHA = (2 * DEPTH) ** 0.25
BETA = (8 * DEPTH) ** -0.25
IN_Q_NSA = NSA_HEADS * NSA_HEAD_DIM
IN_KV_NSA = 6 * NSA_KV_HEADS * NSA_HEAD_DIM
IN_GATE = NSA_HEADS * 3
IN_DIL = DIL_GROUPS * DIL_HEADS * DIL_HEAD_DIM
IN_COLS = IN_Q_NSA + IN_KV_NSA + IN_GATE + 3 * IN_DIL
NEG = -1e30
TINY = 1e-30
FORCED_SCORE = 1e4

kernel_name = 'nsa_dilated_hier_moe_decoder_step'

def layer_norm(x, g, b):
    xf = x.astype(jnp.float32)
    mu = jnp.mean(xf, -1, keepdims=True)
    var = jnp.mean(jnp.square(xf - mu), -1, keepdims=True)
    return ((xf - mu) * lax.rsqrt(var + 1e-5) * g + b).astype(x.dtype)

def t5_bucket(dist):
    n = jnp.maximum(dist, 0)
    exact = NUM_BUCKETS // 2
    nf = jnp.maximum(n, 1).astype(jnp.float32)
    large = exact + (jnp.log(nf / exact) / math.log(MAX_DISTANCE / exact) * (NUM_BUCKETS - exact)).astype(jnp.int32)
    large = jnp.minimum(large, NUM_BUCKETS - 1)
    return jnp.where(n < exact, n, large)

def masked_softmax(s, valid):
    s = jnp.where(valid, s, NEG)
    m = jnp.max(s, -1, keepdims=True)
    e = jnp.where(valid, jnp.exp(s - m), 0.0)
    den = jnp.maximum(jnp.sum(e, -1, keepdims=True), TINY)
    return e / den, (m + jnp.log(den))[..., 0]

def banded_attention(q, k, v, window, stride, tbl):
    n, length, hk, g, hd = q.shape
    nb = -(-length // Q_BLOCK)
    pad = nb * Q_BLOCK - length
    kwin = Q_BLOCK + window
    qp = jnp.pad(q, ((0, 0), (0, pad), (0, 0), (0, 0), (0, 0)))
    kp = jnp.pad(k, ((0, 0), (window, pad), (0, 0), (0, 0)))
    vp = jnp.pad(v, ((0, 0), (window, pad), (0, 0), (0, 0)))
    idx = jnp.arange(nb)[:, None] * Q_BLOCK + jnp.arange(kwin)[None, :]
    ks = jnp.swapaxes(kp[:, idx], 0, 1)
    vs = jnp.swapaxes(vp[:, idx], 0, 1)
    qs = jnp.swapaxes(qp.reshape(n, nb, Q_BLOCK, hk, g, hd), 0, 1)
    du = jnp.arange(Q_BLOCK)[:, None] - jnp.arange(kwin)[None, :] + window
    valid = (du >= 0) & (du <= window) & ((idx - window)[:, None, :] >= 0)
    bias = tbl[:, :, t5_bucket(du * stride)].astype(jnp.float32)
    scale = hd ** -0.5

    def one_block(args):
        qb, kb, vb, mask = args
        s = jnp.einsum('nqhgd,nkhd->nhgqk', qb, kb, preferred_element_type=jnp.float32) * scale + bias
        p, lse = masked_softmax(s, mask)
        o = jnp.einsum('nhgqk,nkhd->nqhgd', p, vb.astype(jnp.float32))
        return o, jnp.transpose(lse, (0, 3, 1, 2))

    o, lse = lax.map(one_block, (qs, ks, vs, valid))
    o = jnp.swapaxes(o, 0, 1).reshape(n, nb * Q_BLOCK, hk, g, hd)[:, :length]
    lse = jnp.swapaxes(lse, 0, 1).reshape(n, nb * Q_BLOCK, hk, g)[:, :length]
    return o, lse

def dilated_prompt(q, k, v, window, dil, tbl):
    b, s, h, d = q.shape

    def by_residue(t):
        return t.reshape(b, s // dil, dil, h, d).transpose(0, 2, 1, 3, 4).reshape(b * dil, s // dil, h, d)

    o, lse = banded_attention(by_residue(q)[:, :, :, None], by_residue(k), by_residue(v), window // dil, dil, tbl[:, None])
    o = o[:, :, :, 0].reshape(b, dil, s // dil, h, d).transpose(0, 2, 1, 3, 4).reshape(b, s, h, d)
    lse = lse[..., 0].reshape(b, dil, s // dil, h).transpose(0, 2, 1, 3).reshape(b, s, h)
    return o, lse

def dilated_sample(q, k_new, v_new, buf, window, dil, tbl):
    length = buf.shape[1]
    ds = q.shape[1]
    kcat = jnp.concatenate([buf[:, :, 0], k_new.astype(buf.dtype)], 1)
    vcat = jnp.concatenate([buf[:, :, 1], v_new.astype(buf.dtype)], 1)
    tpos = PAST_LEN + jnp.arange(ds)
    steps = jnp.arange(window // dil + 1) * dil
    idx = tpos[:, None] - steps[None, :] - (PAST_LEN - length)
    valid = idx >= 0
    idxc = jnp.maximum(idx, 0)
    kg = kcat[:, idxc]
    vg = vcat[:, idxc]
    bias = tbl[:, t5_bucket(steps)].astype(jnp.float32)
    s = jnp.einsum('bqhd,bqkhd->bhqk', q, kg, preferred_element_type=jnp.float32) * (q.shape[-1] ** -0.5) + bias[:, None, :]
    p, lse = masked_softmax(s, valid)
    o = jnp.einsum('bhqk,bqkhd->bqhd', p, vg.astype(jnp.float32))
    return o, jnp.swapaxes(lse, 1, 2)

def combine_dilations(outs, lses):
    w = jax.nn.softmax(jnp.stack(lses, 0).astype(jnp.float32), axis=0)
    return jnp.sum(w[..., None] * jnp.stack(outs, 0), 0)

def compress(k, pool):
    b, t, kvh, d = k.shape
    n_sub = t // CMP_STRIDE
    sub = k[:, :n_sub * CMP_STRIDE].reshape(b, n_sub, CMP_STRIDE, kvh, d)
    first = jnp.einsum('bnjhd,jh->bnhd', sub, pool[:CMP_STRIDE])
    second = jnp.einsum('bnjhd,jh->bnhd', sub, pool[CMP_STRIDE:])
    return first[:, :-1] + second[:, 1:]

def to_blocks(k):
    b, t, kvh, d = k.shape
    ns = -(-t // SEL_LEN)
    kp = jnp.pad(k, ((0, 0), (0, ns * SEL_LEN - t), (0, 0), (0, 0)))
    return kp.reshape(b, ns, SEL_LEN, kvh, d).transpose(0, 3, 1, 2, 4)

def nsa_cmp_sel(q, q_pos, kc, vc, kb, vb, tbl):
    b, nq, kvh = q.shape[:3]
    n_cmp = kc.shape[1]
    n_sel = kb.shape[2]
    scale = NSA_HEAD_DIM ** -0.5
    cmp_start = jnp.arange(n_cmp) * CMP_STRIDE
    dist_c = q_pos[:, None] - (cmp_start + CMP_LEN - 1)[None, :]
    s = jnp.einsum('bqhgd,bnhd->bhgqn', q, kc, preferred_element_type=jnp.float32) * scale + tbl[:, :, t5_bucket(dist_c)]
    p_c, _ = masked_softmax(s, dist_c >= 0)
    o_c = jnp.einsum('bhgqn,bnhd->bqhgd', p_c, vc.astype(jnp.float32))
    sel_start = jnp.arange(n_sel) * SEL_LEN
    overlap = ((cmp_start[:, None] < sel_start[None, :] + SEL_LEN)
               & (cmp_start[:, None] + CMP_LEN > sel_start[None, :])).astype(jnp.float32)
    imp = jnp.einsum('bhgqn,ns->bhqs', p_c, overlap)
    cur = (q_pos // SEL_LEN)[:, None]
    blk = jnp.arange(n_sel)[None, :]
    forced = (blk == 0) | (blk == cur) | (blk == cur - 1)
    causal = sel_start[None, :] <= q_pos[:, None]
    imp = jnp.where(causal, jnp.where(forced, FORCED_SCORE, imp), NEG)
    _, top_idx = lax.top_k(imp, min(SEL_TOP_N, n_sel))
    gather = jax.vmap(jax.vmap(lambda blocks, ix: blocks[ix]))
    kg = gather(kb, top_idx).reshape(b, kvh, nq, -1, NSA_HEAD_DIM)
    vg = gather(vb, top_idx).reshape(b, kvh, nq, -1, NSA_HEAD_DIM)
    kpos = (top_idx[..., None] * SEL_LEN + jnp.arange(SEL_LEN)).reshape(b, kvh, nq, -1)
    dist_s = q_pos[None, None, :, None] - kpos
    tbl_r = jnp.transpose(tbl, (0, 2, 1))
    bias = jnp.moveaxis(tbl_r[jnp.arange(kvh)[None, :, None, None], t5_bucket(dist_s)], -1, 2)
    s2 = jnp.einsum('bqhgd,bhqkd->bhgqk', q, kg, preferred_element_type=jnp.float32) * scale + bias
    p_s, _ = masked_softmax(s2, (dist_s >= 0)[:, :, None])
    o_s = jnp.einsum('bhgqk,bhqkd->bqhgd', p_s, vg.astype(jnp.float32))
    return o_c, o_s

def window_sample(q, k_new, v_new, buf, tbl):
    length = buf.shape[1]
    ds = q.shape[1]
    kcat = jnp.concatenate([buf[:, :, 0], k_new.astype(buf.dtype)], 1)
    vcat = jnp.concatenate([buf[:, :, 1], v_new.astype(buf.dtype)], 1)
    kpos = PAST_LEN - length + jnp.arange(length + ds)
    dist = (PAST_LEN + jnp.arange(ds))[:, None] - kpos[None, :]
    valid = (dist >= 0) & (dist <= NSA_WINDOW)
    s = jnp.einsum('bqhgd,bkhd->bhgqk', q, kcat, preferred_element_type=jnp.float32) * (NSA_HEAD_DIM ** -0.5) + tbl[:, :, t5_bucket(dist)]
    p, _ = masked_softmax(s, valid)
    return jnp.einsum('bhgqk,bkhd->bqhgd', p, vcat.astype(jnp.float32))

def split_projection(proj):
    b, nq = proj.shape[:2]
    o1 = IN_Q_NSA
    o2 = o1 + IN_KV_NSA
    o3 = o2 + IN_GATE
    o4 = o3 + IN_DIL
    o5 = o4 + IN_DIL
    q_n = proj[..., :o1].reshape(b, nq, NSA_KV_HEADS, NSA_GROUP, NSA_HEAD_DIM)
    kv6 = proj[..., o1:o2].reshape(b, nq, 6, NSA_KV_HEADS, NSA_HEAD_DIM)
    gate = jax.nn.sigmoid(proj[..., o2:o3].astype(jnp.float32)).reshape(b, nq, NSA_KV_HEADS, NSA_GROUP, 3)
    qd = proj[..., o3:o4].reshape(b, nq, DIL_GROUPS, DIL_HEADS, DIL_HEAD_DIM)
    kd = proj[..., o4:o5].reshape(b, nq, DIL_GROUPS, DIL_HEADS, DIL_HEAD_DIM)
    vd = proj[..., o5:].reshape(b, nq, DIL_GROUPS, DIL_HEADS, DIL_HEAD_DIM)
    return q_n, kv6, gate, qd, kd, vd

def nsa_merge(o_c, o_s, o_w, gate):
    o = gate[..., 0:1] * o_c + gate[..., 1:2] * o_s + gate[..., 2:3] * o_w
    return o.reshape(o.shape[0], o.shape[1], IN_Q_NSA)

def prompt_mixer(proj, cmp_pool, tbl_nsa, tbl_dil):
    b, s = proj.shape[:2]
    q_n, kv6, gate, qd, kd, vd = split_projection(proj)
    kc = compress(kv6[:, :, 0], cmp_pool[0])
    vc = compress(kv6[:, :, 1], cmp_pool[1])
    kb = to_blocks(kv6[:, :, 2])
    vb = to_blocks(kv6[:, :, 3])
    nb = s // Q_BLOCK
    q_blocks = jnp.swapaxes(q_n.reshape(b, nb, Q_BLOCK, NSA_KV_HEADS, NSA_GROUP, NSA_HEAD_DIM), 0, 1)
    pos_blocks = jnp.arange(s).reshape(nb, Q_BLOCK)
    o_c, o_s = lax.map(lambda a: nsa_cmp_sel(a[0], a[1], kc, vc, kb, vb, tbl_nsa), (q_blocks, pos_blocks))
    o_c = jnp.swapaxes(o_c, 0, 1).reshape(b, s, NSA_KV_HEADS, NSA_GROUP, NSA_HEAD_DIM)
    o_s = jnp.swapaxes(o_s, 0, 1).reshape(b, s, NSA_KV_HEADS, NSA_GROUP, NSA_HEAD_DIM)
    o_w, _ = banded_attention(q_n, kv6[:, :, 4], kv6[:, :, 5], NSA_WINDOW, 1, tbl_nsa)
    o_nsa = nsa_merge(o_c, o_s, o_w, gate)
    outs, lses, dil_states = [], [], []
    for gi, (win, dil) in enumerate(DIL_CONFIGS):
        o, lse = dilated_prompt(qd[:, :, gi], kd[:, :, gi], vd[:, :, gi], win, dil, tbl_dil[gi])
        outs.append(o)
        lses.append(lse)
        keep = min(win, s)
        dil_states.append(jnp.stack([kd[:, -keep:, gi], vd[:, -keep:, gi]], 2))
    o_dil = combine_dilations(outs, lses).reshape(b, s, DIL_HEADS * DIL_HEAD_DIM)
    mix = jnp.concatenate([o_nsa, o_dil], -1).astype(proj.dtype)
    state = (kv6[:, :, :4], kv6[:, -min(NSA_WINDOW, s):, 4:], dil_states[0], dil_states[1], dil_states[2])
    return mix, state

def sample_mixer(proj, layer, cache_nsa, cache_win, buf0, buf1, buf2, page_table, cmp_pool, tbl_nsa, tbl_dil):
    db, ds = proj.shape[:2]
    q_n, kv6, gate, qd, kd, vd = split_projection(proj)
    past_len = page_table.shape[1] * PAGE_SIZE
    past = cache_nsa[layer, page_table].reshape(db, past_len, 4, NSA_KV_HEADS, NSA_HEAD_DIM)
    full = jnp.concatenate([past, kv6[:, :, :4].astype(past.dtype)], 1)
    kc = compress(full[:, :, 0], cmp_pool[0])
    vc = compress(full[:, :, 1], cmp_pool[1])
    kb = to_blocks(full[:, :, 2])
    vb = to_blocks(full[:, :, 3])
    q_pos = PAST_LEN + jnp.arange(ds)
    o_c, o_s = nsa_cmp_sel(q_n, q_pos, kc, vc, kb, vb, tbl_nsa)
    o_w = window_sample(q_n, kv6[:, :, 4], kv6[:, :, 5], cache_win, tbl_nsa)
    o_nsa = nsa_merge(o_c, o_s, o_w, gate)
    outs, lses, dil_states = [], [], []
    for gi, ((win, dil), buf) in enumerate(zip(DIL_CONFIGS, (buf0, buf1, buf2))):
        o, lse = dilated_sample(qd[:, :, gi], kd[:, :, gi], vd[:, :, gi], buf, win, dil, tbl_dil[gi])
        outs.append(o)
        lses.append(lse)
        new_rows = jnp.stack([kd[:, :, gi], vd[:, :, gi]], 2).astype(buf.dtype)
        dil_states.append(jnp.concatenate([buf, new_rows], 1)[:, -buf.shape[1]:])
    o_dil = combine_dilations(outs, lses).reshape(db, ds, DIL_HEADS * DIL_HEAD_DIM)
    mix = jnp.concatenate([o_nsa, o_dil], -1).astype(proj.dtype)
    new_win = jnp.concatenate([cache_win, kv6[:, :, 4:].astype(cache_win.dtype)], 1)[:, -cache_win.shape[1]:]
    state = (kv6[:, :, :4], new_win, dil_states[0], dil_states[1], dil_states[2])
    return mix, state

def hier_moe(h, w_rg, b_rg, w_re, b_re, w_gu, w_dn):
    b, nq, d = h.shape
    hf = h.reshape(b * nq, d)
    lg = (hf @ w_rg + b_rg).astype(jnp.float32)
    pg = jax.nn.softmax(lg, -1)
    gsel = jnp.argmax(lg, -1)
    pg_sel = jnp.take_along_axis(pg, gsel[:, None], -1)
    le = (hf @ w_re + b_re).astype(jnp.float32).reshape(-1, N_EXPERT_GROUPS, EXPERTS_PER_GROUP)
    le_sel = jnp.take_along_axis(le, gsel[:, None, None], 1)[:, 0]
    top_v, top_i = lax.top_k(le_sel, TOP_K_EXPERT)
    w = pg_sel * jax.nn.softmax(top_v, -1)
    eid = gsel[:, None] * EXPERTS_PER_GROUP + top_i
    gates = jnp.einsum('nke,nk->ne', jax.nn.one_hot(eid, N_EXPERTS, dtype=jnp.float32), w)
    gu = jnp.einsum('nd,edf->nef', hf, w_gu)
    hid = jax.nn.silu(gu[..., :D_EXPERT]) * gu[..., D_EXPERT:] * gates[..., None].astype(gu.dtype)
    y = jnp.einsum('nef,efd->nd', hid, w_dn)
    return y.reshape(b, nq, d).astype(h.dtype)

def trunk_layer(x, c, mixer, w_ada, b_ada, w_in, w_o, ln_g, ln_b, w_rg, b_rg, w_re, b_re, w_gu, w_dn):
    mod = jax.nn.silu(c) @ w_ada + b_ada
    sh1, sc1, g1, sh2, sc2, g2 = jnp.split(mod[:, None, :], 6, axis=-1)
    h = x * (1 + sc1) + sh1
    mix, state = mixer(h @ w_in)
    a = mix.astype(x.dtype) @ w_o
    x = layer_norm(ALPHA * x + (1 + g1) * a, ln_g[0], ln_b[0])
    h = x * (1 + sc2) + sh2
    f = hier_moe(h, w_rg, b_rg, w_re, b_re, w_gu, w_dn)
    x = layer_norm(ALPHA * x + (1 + g2) * f, ln_g[1], ln_b[1])
    return x, state

def setup_inputs(seed: int = 0) -> dict:
    key = jax.random.key(seed)
    ks = jax.random.split(key, 26)
    n_pages = PAST_LEN // PAGE_SIZE
    n_used = DEC_BATCH * n_pages
    n_pool = n_used + max(1, n_used // 4)
    f32 = jnp.float32
    nrm = lambda k, shape, s=1.0: s * jax.random.normal(k, shape, f32)
    page_table = jax.random.permutation(ks[0], n_pool)[:n_used].reshape(DEC_BATCH, n_pages).astype(jnp.int32)
    dil_caches = [nrm(ks[5 + i], (DEPTH, DEC_BATCH, min(w, PAST_LEN), 2, DIL_HEADS, DIL_HEAD_DIM)) for i, (w, _) in enumerate(DIL_CONFIGS)]
    return {
        'x_prompt': nrm(ks[1], (BATCH, SEQ, D_MODEL)),
        'x_sample': nrm(ks[2], (DEC_BATCH, DEC_SEQ, D_MODEL)),
        'cache_nsa': nrm(ks[3], (DEPTH, n_pool, PAGE_SIZE, 4, NSA_KV_HEADS, NSA_HEAD_DIM)),
        'cache_nsa_win': nrm(ks[4], (DEPTH, DEC_BATCH, min(NSA_WINDOW, PAST_LEN), 2, NSA_KV_HEADS, NSA_HEAD_DIM)),
        'cache_dil0': dil_caches[0],
        'cache_dil1': dil_caches[1],
        'cache_dil2': dil_caches[2],
        'page_table': page_table,
        'c_prompt': nrm(ks[8], (BATCH, D_MODEL)),
        'c_sample': nrm(ks[9], (DEC_BATCH, D_MODEL)),
        'rel_bias': nrm(ks[10], (NUM_BUCKETS, N_ATT_HEADS), 0.3),
        'w_ada': nrm(ks[11], (DEPTH, D_MODEL, 6 * D_MODEL), 0.2 * D_MODEL ** -0.5),
        'b_ada': nrm(ks[12], (DEPTH, 6 * D_MODEL), 0.02),
        'w_in': nrm(ks[13], (DEPTH, D_MODEL, IN_COLS), D_MODEL ** -0.5),
        'cmp_pool': (1.0 + nrm(ks[14], (DEPTH, 2, CMP_LEN, NSA_KV_HEADS), 0.1)) / CMP_LEN,
        'w_o': nrm(ks[15], (DEPTH, MIX_WIDTH, D_MODEL), BETA * MIX_WIDTH ** -0.5),
        'ln_g': 1.0 + nrm(ks[16], (DEPTH, 2, D_MODEL), 0.02),
        'ln_b': nrm(ks[17], (DEPTH, 2, D_MODEL), 0.02),
        'w_router_group': nrm(ks[18], (DEPTH, D_MODEL, N_EXPERT_GROUPS), D_MODEL ** -0.5),
        'b_router_group': nrm(ks[19], (DEPTH, N_EXPERT_GROUPS), 0.01),
        'w_router_expert': nrm(ks[20], (DEPTH, D_MODEL, N_EXPERTS), D_MODEL ** -0.5),
        'b_router_expert': nrm(ks[21], (DEPTH, N_EXPERTS), 0.01),
        'w_gate_up': nrm(ks[22], (DEPTH, N_EXPERTS, D_MODEL, 2 * D_EXPERT), D_MODEL ** -0.5),
        'w_down': nrm(ks[23], (DEPTH, N_EXPERTS, D_EXPERT, D_MODEL), BETA * D_EXPERT ** -0.5),
    }

def reference(x_prompt, x_sample, cache_nsa, cache_nsa_win, cache_dil0, cache_dil1, cache_dil2, page_table,
              c_prompt, c_sample, rel_bias, w_ada, b_ada, w_in, cmp_pool, w_o, ln_g, ln_b,
              w_router_group, b_router_group, w_router_expert, b_router_expert, w_gate_up, w_down):
    tbl_nsa = rel_bias[:, :NSA_HEADS].T.reshape(NSA_KV_HEADS, NSA_GROUP, NUM_BUCKETS)
    tbl_dil = rel_bias[:, NSA_HEADS:].T.reshape(DIL_GROUPS, DIL_HEADS, NUM_BUCKETS)
    xp, xs = x_prompt, x_sample
    states_p, states_s = [], []
    for l in range(DEPTH):
        layer_w = (w_ada[l], b_ada[l], w_in[l], w_o[l], ln_g[l], ln_b[l], w_router_group[l], b_router_group[l],
                   w_router_expert[l], b_router_expert[l], w_gate_up[l], w_down[l])
        mix_p = functools.partial(prompt_mixer, cmp_pool=cmp_pool[l], tbl_nsa=tbl_nsa, tbl_dil=tbl_dil)
        mix_s = functools.partial(sample_mixer, layer=l, cache_nsa=cache_nsa, cache_win=cache_nsa_win[l],
                                  buf0=cache_dil0[l], buf1=cache_dil1[l], buf2=cache_dil2[l], page_table=page_table,
                                  cmp_pool=cmp_pool[l], tbl_nsa=tbl_nsa, tbl_dil=tbl_dil)
        xp, sp = trunk_layer(xp, c_prompt, mix_p, *layer_w)
        xs, ss = trunk_layer(xs, c_sample, mix_s, *layer_w)
        states_p.append(sp)
        states_s.append(ss)
    nsa_p, win_p, d0_p, d1_p, d2_p = [jnp.stack(a) for a in zip(*states_p)]
    nsa_s, win_s, d0_s, d1_s, d2_s = [jnp.stack(a) for a in zip(*states_s)]
    return (xp, xs, nsa_p, nsa_s, win_p, win_s, d0_p, d0_s, d1_p, d1_s, d2_p, d2_s)


_drawn_inputs = setup_inputs


def setup_inputs(seed=0):
    import zlib

    import numpy as np

    out = dict(_drawn_inputs(seed))
    spreads = {}
    factors = {'rel_bias': 2.794, 'cmp_pool': 8.0, 'b_router_group': 5.099, 'b_router_expert': 18.889}
    for name, (base, spread) in spreads.items():
        noise = np.random.default_rng([zlib.crc32(name.encode()), seed]).standard_normal(out[name].shape)
        drawn = base * np.exp(spread * noise) if base else spread * noise
        out[name] = __import__('jax').numpy.asarray(drawn.astype(out[name].dtype))
    for name, factor in factors.items():
        out[name] = (out[name] * factor).astype(out[name].dtype)
    return out
```

```python
import math
from contextlib import ExitStack

import numpy as np
import concourse.bass as bass
from concourse import mybir

F32 = mybir.dt.float32
U32 = mybir.dt.uint32
I32 = mybir.dt.int32
ALU = mybir.AluOpType
ACT = mybir.ActivationFunctionType
AX = mybir.AxisListType

P = 128
D = 2048
KT = D // P
SEQ = 512
DB, DS = 8, 4
NS = DB * DS
TOK = SEQ + NS
TT = [(t * P, min(P, TOK - t * P)) for t in range((TOK + P - 1) // P)]
NTT = len(TT)
PAST = 2048
PAGE = 128
N_PAGES = PAST // PAGE
HD, NH, KV, G = 64, 24, 4, 6
DHD, DH, NG = 128, 4, 3
DIL = ((128, 1), (512, 4), (2048, 16))
NBKT = 32
C_Q = 0
C_KV = NH * HD
C_GATE = C_KV + 6 * KV * HD
C_DQ = C_GATE + 3 * NH
C_DK = C_DQ + NG * DH * DHD
C_DV = C_DK + NG * DH * DHD
COLS = C_DV + NG * DH * DHD
BLK = 512
NBLK = (COLS + BLK - 1) // BLK
LASTW = COLS - (NBLK - 1) * BLK
NE, DE = 16, 256
ALPHA = 2 ** 0.25
NEG = -1e30
TINY = 1e-30
FORCED = 1e4
EPS = 1e-5
R_NSA = 1023
W_NSA = 896
R_DIL = 383
W_DIL = 256


def t5_bucket(dist):
    n = np.maximum(dist, 0)
    exact = NBKT // 2
    nf = np.maximum(n, 1).astype(np.float32)
    large = exact + (np.log(nf / np.float32(exact)) / np.float32(math.log(128 / exact)) * np.float32(NBKT - exact)).astype(np.int32)
    return np.where(n < exact, n, np.minimum(large, NBKT - 1))


def one_hot(dist, valid):
    dist, valid = np.broadcast_arrays(dist, valid)
    dist, valid = dist.ravel(), valid.ravel()
    out = np.zeros((NBKT + 1, dist.size), np.float32)
    at = np.where(valid, t5_bucket(dist), NBKT)
    out[at, np.arange(dist.size)] = 1.0
    return out


def shape_tables():
    i = np.arange
    du = 511 - i(R_NSA)
    tabs = {"oh_nsa": one_hot(du, du >= 0)}
    du = 255 - i(R_DIL)
    tabs["oh_dil"] = np.stack([one_hot(du * dil, (du >= 0) & (du <= P)) for _, dil in DIL], 1).reshape(NBKT + 1, NG * R_DIL)
    tabs["ident"] = np.eye(P, dtype=np.float32)
    res = i(P) // 32
    tabs["res_mask"] = np.where(res[:, None] == res[None, :], 0.0, NEG).astype(np.float32)
    q = i(DS)[:, None]
    col = i(PAST)[None, :]
    sel = one_hot(PAST + q - col, True).reshape(NBKT + 1, DS, PAST)
    win = one_hot(512 + q - (4 * (i(512) % P) + i(512) // P)[None, :], ((512 + q - (4 * (i(512) % P) + i(512) // P)[None, :]) <= 512)).reshape(NBKT + 1, DS, 512)
    cmp_ = one_hot(PAST + q - (16 * i(P) + 31)[None, :], (i(P) < P - 1)[None, :]).reshape(NBKT + 1, DS, P)
    t = i(NS + 28)[None, :] - 28
    new = one_hot(q - t, (t >= 0) & (t <= q)).reshape(NBKT + 1, DS, NS + 28)
    tabs["oh_smp"] = np.concatenate([sel, win, cmp_, new], 2).reshape(NBKT + 1, -1)
    t, j, m = i(P)[None, None, :], i(32)[:, None, None], i(9)[None, :, None]
    tabs["oh_pool"] = (j == t - 16 * (m - 1)).astype(np.float32).reshape(32, 9 * P)
    tabs["rowid"] = i(P).astype(np.float32)[:, None]
    r = i(P)
    ok = (r % 32) < 24
    same = (r[:, None] // 32 == r[None, :] // 32) & (r[:, None] % 4 == r[None, :] % 4) & ok[:, None] & ok[None, :]
    tabs["group_sum"] = same.astype(np.float32)
    blk = i(33)
    cs = i(P)[:, None] * 16
    ov = (cs < blk[None, :] * 64 + 64) & (cs + 32 > blk[None, :] * 64) & (i(P)[:, None] < P - 1)
    tabs["overlap"] = ov.astype(np.float32)
    forced = np.isin(blk, (0, 31, 32)).astype(np.float32)
    tabs["forced"] = np.broadcast_to(np.concatenate([1 - forced, forced * FORCED]), (P, 66)).astype(np.float32).copy()
    tq = i(NS) % DS
    parts = []
    for g, (_, dil) in enumerate(DIL):
        m = i(P)[None, :]
        if dil == 1:
            dist = P + q - m
            old = one_hot(dist, dist <= P)
            new = one_hot(q - tq[None, :], q >= tq[None, :])
        else:
            old = one_hot(np.broadcast_to((P - m) * dil, (DS, P)), True)
            new = one_hot(np.zeros((DS, NS), np.int64), q == tq[None, :])
        parts.append(np.concatenate([old.reshape(NBKT + 1, DS, P), new.reshape(NBKT + 1, DS, NS)], 2))
    tabs["oh_ds"] = np.stack(parts, 1).reshape(NBKT + 1, NG * DS * 160)
    rb = (i(P) % NS) // DS
    tabs["batch_mask"] = np.where(rb[:, None] == (i(NS) // DS)[None, :], 0.0, NEG).astype(np.float32)
    tabs["first"] = np.broadcast_to(np.arange(16, 0, -1), (P, 16)).astype(np.float32).copy()
    return tabs


class Prog:

    def __init__(self, nc, ins, outs):
        self.nc, self.i, self.o = nc, ins, outs
        self.ctx = ExitStack()
        self.phase = None
        self.ring = self.sb("ring", [P, 4, 8, BLK])
        self.xt = self.sb("xt", [P, KT, TOK])
        self.ident = self.sb("ident_sb", [P, P])
        self.dilT = self.sb("dilT", [P, DH, NS])
        self.ring_full = [self.sem(f"ring_full{s}") for s in range(4)]
        self.ring_used = self.sem("ring_used")
        self.copied = self.sem("copied")
        self.tab_out = self.sem("tab_out")
        self.copies = 0
        self.banks = [self.ctx.enter_context(nc.psum_tensor(f"bank{i}", [P, 512], F32)) for i in range(8)]
        self.proj = nc.dram_tensor("proj", [TOK, COLS], F32).ap()
        self.modd = nc.dram_tensor("modd", [9, 4 * D], F32).ap()
        self.mixd = nc.dram_tensor("mixd", [TOK, D], F32).ap()
        self.od = nc.dram_tensor("od", [NG, SEQ, DH, 130], F32).ap()
        self.ad = nc.dram_tensor("ad", [TOK, D], F32).ap()
        self.yd = nc.dram_tensor("yd", [TOK, D], F32).ap()
        self.x1d = nc.dram_tensor("x1d", [TOK, D], F32).ap()
        self.gated = nc.dram_tensor("gated", [NE, TOK], F32).ap()
        self.tabn = nc.dram_tensor("tabn", [NH, P * R_NSA + P], F32)
        self.tabd = nc.dram_tensor("tabd", [NG * DH, P * R_DIL + P], F32)

    def sb(self, name, shape, dt=F32, ctx=None):
        return (ctx or self.ctx).enter_context(self.nc.sbuf_tensor(name, shape, dt))

    def sem(self, name, ctx=None):
        sem = self.nc.alloc_semaphore(name)
        if ctx is not None:
            if self.phase is not ctx:
                self.phase, own = ctx, []
                self.own = own
                ctx.callback(self.nc.all_engine_barrier)
                ctx.callback(lambda: self.nc.clear_and_free_semaphores(own))
            self.own.append(sem)
        return sem

    def load_half(self, eng, slot, w, row0, col0, width=BLK, wait=None):
        if wait is not None:
            eng.wait_ge(self.ring_used, wait)
        src = w[row0:row0 + 8 * P, bass.ds(col0, width)].rearrange("(t p) c -> p t c", p=P)
        eng.dma_start(self.ring[:, slot, :, 0:width], src).then_inc(self.ring_full[slot], 16)


def phase_ada(R, w_ada, w_in):
    nc, I = R.nc, R.i
    NB = 6 * D // BLK
    with ExitStack() as ctx:
        mod = R.sb("mod", [9, 6 * D], ctx=ctx)
        cs = R.sb("cs", [9, D], ctx=ctx)
        ct = R.sb("ct", [P, KT, 9], ctx=ctx)
        modt = R.sb("modt", [P, 2 * KT, 9], ctx=ctx)
        sc_s = R.sb("sc_s", [P, 2, KT, NS], ctx=ctx)
        xn = R.sb("xn", [P, 2, D], ctx=ctx)
        c_in = R.sem("c_in", ctx)
        b_in = R.sem("b_in", ctx)
        id_in = R.sem("id_in", ctx)
        x_in = [R.sem(f"x_in{s}", ctx) for s in range(2)]
        silu_done = R.sem("silu_done", ctx)
        ct_ps = R.sem("ct_ps", ctx)
        ct_ready = R.sem("ct_ready", ctx)
        xT_ps = R.sem("xT_ps", ctx)
        xT_done = R.sem("xT_done", ctx)
        mod_done = R.sem("mod_done", ctx)
        modT_ps = R.sem("modT_ps", ctx)
        modT_done = R.sem("modT_done", ctx)
        sc_done = R.sem("sc_done", ctx)
        modd_out = R.sem("modd_out", ctx)
        block = ctx.enter_context(nc.Block())
        ps_mod, ps_x = R.banks[0:2], R.banks[2:4]

        @block.sync
        def _(eng):
            for n in range(4):
                R.load_half(eng, n, w_ada, (n % 2) * 8 * P, (n // 2) * BLK)
            with eng.Fori(1, NB // 2) as it:
                for s in range(4):
                    R.load_half(eng, s, w_ada, (s % 2) * 8 * P, (2 * it + s // 2) * BLK, wait=4 * it + s - 3)
            for s in range(4):
                R.load_half(eng, s, w_in, (s % 2) * 8 * P, (s // 2) * BLK, wait=2 * NB - 3 + s)

        @block.gpsimd
        def _(eng):
            eng.dma_start(cs[0:1, :], I["c_prompt"]).then_inc(c_in, 16)
            eng.dma_start(cs[1:9, :], I["c_sample"]).then_inc(c_in, 16)
            eng.dma_start(R.ident[:, :], I["ident"]).then_inc(id_in, 16)
            for t, (t0, n) in enumerate(TT):
                if t >= 2:
                    eng.wait_ge(xT_ps, 4 * (t - 1))
                src = I["x_prompt"][0, t0:t0 + n, :] if t < 4 else I["x_sample"].rearrange("b q d -> (b q) d")
                eng.dma_start(xn[0:n, t % 2, :], src).then_inc(x_in[t % 2], 16)
            eng.dma_start(mod[:, :], I["b_ada"].to_broadcast([9, 6 * D])).then_inc(b_in, 16)
            eng.wait_ge(mod_done, NB + 2)
            eng.dma_start(R.modd, mod[:, 2 * D:6 * D]).then_inc(modd_out, 16)
            eng.wait_ge(modd_out, 16)

        @block.scalar
        def _(act):
            act.wait_ge(c_in, 32)
            act.activation(cs[:, :], cs[:, :], ACT.Silu).then_inc(silu_done, 1)
            for t, (t0, n) in enumerate(TT):
                for j in range(4):
                    u = 4 * t + j
                    act.wait_ge(xT_ps, u + 1)
                    act.activation(R.xt[:, 4 * j:4 * j + 4, t0:t0 + n],
                                   ps_x[u % 2][:, 0:4 * n].rearrange("p (k n) -> p k n", n=n), ACT.Copy).then_inc(xT_done, 1)

        @block.tensor
        def _(pe):
            pe.wait_ge(silu_done, 1)
            pe.wait_ge(id_in, 16)
            for k in range(KT):
                last = pe.transpose(ps_mod[0][:, 9 * k:9 * k + 9], cs[:, k * P:(k + 1) * P], R.ident[0:9, 0:9])
            last.then_inc(ct_ps, 1)
            for t, (t0, n) in enumerate(TT):
                pe.wait_ge(x_in[t % 2], 16 * (t // 2 + 1))
                for j in range(4):
                    u = 4 * t + j
                    if u >= 2:
                        pe.wait_ge(xT_done, u - 1)
                    for k in range(4):
                        last = pe.transpose(ps_x[u % 2][:, k * n:(k + 1) * n],
                                            xn[0:n, t % 2, (4 * j + k) * P:(4 * j + k + 1) * P], R.ident[0:n, 0:n])
                    last.then_inc(xT_ps, 1)
            pe.wait_ge(ct_ready, 1)
            pe.sem_inc(mod_done, 2)
            with pe.Fori(0, NB // 2) as it:
                for s in range(4):
                    if s % 2 == 0:
                        pe.wait_ge(mod_done, 2 * it + s // 2 + 1)
                    pe.wait_ge(R.ring_full[s], 16 * it + 16)
                    for k in range(8):
                        last = pe.matmul(ps_mod[s // 2][0:9, :], ct[:, 8 * (s % 2) + k, :], R.ring[:, s, k, :],
                                         start=(s % 2 == 0 and k == 0), stop=(s % 2 == 1 and k == 7))
                    last.then_inc(R.ring_used, 1)
            pe.wait_ge(mod_done, NB + 2)
            pe.wait_ge(xT_done, 4 * NTT)
            for j in range(2 * KT):
                last = pe.transpose(ps_x[0][:, 9 * j:9 * j + 9], mod[:, j * P:(j + 1) * P], R.ident[0:9, 0:9])
            last.then_inc(modT_ps, 1)

        @block.vector
        def _(dve):
            dve.wait_ge(ct_ps, 1)
            dve.tensor_copy(ct[:, :, :], ps_mod[0][:, 0:9 * KT].rearrange("p (k n) -> p k n", n=9)).then_inc(ct_ready, 1)
            dve.wait_ge(b_in, 16)
            with dve.Fori(0, NB // 2) as it:
                for b in range(2):
                    dve.wait_ge(R.ring_used, 4 * it + 2 * b + 2)
                    cols = mod[:, bass.ds((2 * it + b) * BLK, BLK)]
                    dve.tensor_tensor(cols, ps_mod[b][0:9, :], cols, ALU.add).then_inc(mod_done, 1)
            dve.wait_ge(modT_ps, 1)
            ps = ps_x[0][:, 0:18 * KT].rearrange("p (k n) -> p k n", n=9)
            dve.tensor_copy(modt[:, 0:KT, :], ps[:, 0:KT, :]).then_inc(modT_done, 1)
            dve.tensor_scalar(modt[:, KT:2 * KT, :], ps[:, KT:2 * KT, :], 1.0, None, ALU.add).then_inc(modT_done, 1)
            dve.wait_ge(modT_done, 2)
            dve.wait_ge(xT_done, 4 * NTT)
            for k in range(KT):
                dve.tensor_scalar(R.xt[:, k, 0:SEQ], R.xt[:, k, 0:SEQ], modt[:, KT + k, 0:1], modt[:, k, 0:1],
                                  ALU.mult, ALU.add)
            for w in range(2):
                dve.tensor_copy(sc_s[:, w, :, :].rearrange("p k (b q) -> p k b q", q=DS),
                                modt[:, w * KT:(w + 1) * KT, 1:9].unsqueeze(3).to_broadcast([P, KT, DB, DS])).then_inc(sc_done, 1)
            xs = R.xt[:, :, SEQ:TOK]
            dve.wait_ge(sc_done, 2)
            dve.tensor_tensor(xs, xs, sc_s[:, 1, :, :], ALU.mult).then_inc(sc_done, 1)
            dve.wait_ge(sc_done, 3)
            dve.tensor_tensor(xs, xs, sc_s[:, 0, :, :], ALU.add)


def phase_gemm(R, name, lhs, kt, w, n_blocks, last_width, first, out, next_loads, begin=None, beside=None):
    nc = R.nc
    per = kt // 8
    bpr = 4 // per
    rounds = n_blocks // bpr
    with ExitStack() as ctx:
        stage = R.sb(name + "_stage", [P, 2, NTT, BLK], ctx=ctx)
        done = R.sem(name + "_done", ctx)
        evac = R.sem(name + "_evac", ctx)
        stored = [R.sem(f"{name}_out{i}", ctx) for i in range(bpr * NTT)]
        stage_free = R.sem(name + "_stage_free", ctx)
        block = ctx.enter_context(nc.Block())
        looped = rounds - 1 if last_width != BLK else rounds

        def both(eng, body):
            with eng.Fori(0, looped) as it:
                body(it, BLK)
            if looped < rounds:
                body(rounds - 1, last_width)

        @block.sync
        def _(eng):
            def load(it, s, width):
                R.load_half(eng, s, w, (s % per) * 8 * P, (bpr * it + s // per) * BLK, width,
                            wait=4 * (first + it) + s - 3)
            if looped > 1:
                with eng.Fori(1, looped) as it:
                    for s in range(4):
                        load(it, s, BLK)
            if looped < rounds:
                for s in range(4):
                    load(rounds - 1, s, last_width if s // per == bpr - 1 else BLK)
            next_loads(eng, 4 * (first + rounds) - 3)

        @block.tensor
        def _(pe):
            def body(it, last):
                for s in range(4):
                    b = s // per
                    w_ = last if b == bpr - 1 else BLK
                    pe.wait_ge(R.ring_full[s], 16 * (first + it) + 16)
                    for t, (t0, n) in enumerate(TT):
                        if s % per == 0:
                            pe.wait_ge(evac, NTT * (bpr * it + b) + t + 1)
                        for k in range(8):
                            mm = pe.matmul(R.banks[t][0:n, 0:w_], lhs[:, 8 * (s % per) + k, t0:t0 + n], R.ring[:, s, k, 0:w_],
                                           start=(s % per == 0 and k == 0), stop=(s % per == per - 1 and k == 7))
                        if s % per == per - 1 and t < NTT - 1:
                            mm.then_inc(done, 1)
                    mm.then_inc(R.ring_used, 1)
            pe.sem_inc(evac, NTT)
            both(pe, body)

        @block.scalar
        def _(act):
            def body(it, last):
                for b in range(bpr):
                    w_ = last if b == bpr - 1 else BLK
                    nb = bpr * it + b
                    act.wait_ge(stage_free, nb + 1)
                    for t, (t0, n) in enumerate(TT):
                        if t < NTT - 1:
                            act.wait_ge(done, (NTT - 1) * nb + t + 1)
                        else:
                            act.wait_ge(R.ring_used, 4 * first + per * (nb + 1))
                        act.activation(stage[0:n, b, t, 0:w_], R.banks[t][0:n, 0:w_], ACT.Copy).then_inc(evac, 1)
            both(act, body)

        @block.gpsimd
        def _(eng):
            def body(it, last):
                for b in range(bpr):
                    w_ = last if b == bpr - 1 else BLK
                    nb = bpr * it + b
                    for t, (t0, n) in enumerate(TT):
                        eng.wait_ge(evac, NTT * nb + t + 1 + NTT)
                        eng.dma_start(out[t0:t0 + n, bass.ds(nb * BLK, w_)], stage[0:n, b, t, 0:w_]).then_inc(stored[b * NTT + t], 16)
                    for t in range(NTT):
                        eng.wait_ge(stored[b * NTT + t], 16 * it + 16)
                    eng.sem_inc(stage_free, 1)
                if beside:
                    beside(eng, it)
            eng.sem_inc(stage_free, bpr)
            if begin:
                begin(eng)
            both(eng, body)


def phase_bias_rows(R, rown, rowd):
    nc, I = R.nc, R.i
    with ExitStack() as ctx:
        tbl = R.sb("tbl", [NBKT + 1, 36], ctx=ctx)
        ohn = R.sb("ohn", [NBKT + 1, R_NSA], ctx=ctx)
        ohd = R.sb("ohd", [NBKT + 1, NG * R_DIL], ctx=ctx)
        neg_set = R.sem("neg_set", ctx)
        tbl_in = R.sem("tbl_in", ctx)
        in_oh = R.sem("in_oh", ctx)
        rows_ps = R.sem("rows_ps", ctx)
        rows_done = R.sem("rows_done", ctx)
        block = ctx.enter_context(nc.Block())
        B = R.banks

        @block.sync
        def _(eng):
            eng.dma_start(ohn[:, :], I["oh_nsa"]).then_inc(in_oh, 16)
            eng.dma_start(ohd[:, :], I["oh_dil"]).then_inc(in_oh, 16)

        @block.gpsimd
        def _(eng):
            eng.memset(tbl[:, :], NEG).then_inc(neg_set, 1)
            eng.wait_ge(neg_set, 1)
            eng.dma_start(tbl[0:NBKT, :], I["rel_bias"]).then_inc(tbl_in, 16)

        @block.tensor
        def _(pe):
            pe.wait_ge(tbl_in, 16)
            pe.wait_ge(in_oh, 32)
            pe.matmul(B[0][0:NH, 0:512], tbl[:, 0:NH], ohn[:, 0:512], start=True, stop=True).then_inc(rows_ps, 1)
            pe.matmul(B[1][0:NH, 0:511], tbl[:, 0:NH], ohn[:, 512:1023], start=True, stop=True).then_inc(rows_ps, 1)
            for g in range(NG):
                pe.matmul(B[2 + g][0:DH, 0:R_DIL], tbl[:, NH + g * DH:NH + (g + 1) * DH],
                          ohd[:, g * R_DIL:(g + 1) * R_DIL], start=True, stop=True).then_inc(rows_ps, 1)

        @block.vector
        def _(dve):
            for n, (dst, src) in enumerate([(rown[:, 0:512], B[0][0:NH, 0:512]), (rown[:, 512:1023], B[1][0:NH, 0:511])]
                                           + [(rowd[:, g, :], B[2 + g][0:DH, 0:R_DIL]) for g in range(NG)]):
                dve.wait_ge(rows_ps, n + 1)
                dve.tensor_copy(dst, src).then_inc(rows_done, 1)


def spread_bias_rows(R, rown, rowd, eng):
    eng.dma_start(R.tabn.ap()[:, 0:P * R_NSA].rearrange("h (p r) -> h p r", p=P),
                  rown[:, :].unsqueeze(1).to_broadcast([NH, P, R_NSA])).then_inc(R.tab_out, 16)
    for g in range(NG):
        eng.dma_start(R.tabd.ap()[g * DH:(g + 1) * DH, 0:P * R_DIL].rearrange("h (p r) -> h p r", p=P),
                      rowd[:, g, :].unsqueeze(1).to_broadcast([DH, P, R_DIL])).then_inc(R.tab_out, 16)


def phase_compress_prompt(R, W):
    nc, I = R.nc, R.i
    with ExitStack() as ctx:
        cn = R.sb("cn", [32, 16, 512], ctx=ctx)
        prod = R.sb("prod", [32, 16, 512], ctx=ctx)
        pool = R.sb("pool", [32, 2, 32, KV], ctx=ctx)
        fs = R.sb("fs", [32, 2, 512], ctx=ctx)
        in_cn = R.sem("in_cn", ctx)
        fs_step = R.sem("fs_step", ctx)
        cmp_ps = R.sem("cmp_ps", ctx)
        cmp_done = R.sem("cmp_done", ctx)
        block = ctx.enter_context(nc.Block())
        B = R.banks

        @block.sync
        def _(eng):
            eng.dma_start(cn[:, :, :], R.proj[0:SEQ, C_KV:C_KV + 512].rearrange("(n j) c -> n j c", j=16)).then_inc(in_cn, 16)
            for w in range(2):
                eng.dma_start(pool[:, w, :, :].rearrange("p j h -> p (j h)"), I["cmp_pool"][0, w].rearrange("j h -> (j h)").rearrange("(a c) -> a c", a=1).to_broadcast([32, 32 * KV])).then_inc(in_cn, 16)
            eng.wait_ge(R.tab_out, 64)

        @block.tensor
        def _(pe):
            pe.wait_ge(fs_step, 4)
            for pr in range(2):
                for w in range(2):
                    last = pe.matmul(B[5][:, 32 * pr:32 * pr + 31], fs[:, w, pr * P:(pr + 1) * P],
                                     R.ident[0:32, w:w + 31], start=(w == 0), stop=(w == 1))
            for w in range(2):
                last = pe.matmul(B[6][0:31, 0:256], R.ident[0:32, w:w + 31], fs[:, w, 256:512],
                                 start=(w == 0), stop=(w == 1))
            last.then_inc(cmp_ps, 1)

        @block.vector
        def _(dve):
            dve.wait_ge(in_cn, 48)
            for w in range(2):
                if w:
                    dve.wait_ge(fs_step, 2)
                for kv in range(2):
                    tab = pool[:, kv, 16 * w:16 * w + 16, :].unsqueeze(3).to_broadcast([32, 16, KV, HD])
                    x = cn[:, :, 256 * kv:256 * kv + 256].rearrange("p j (h d) -> p j h d", h=KV)
                    y = prod[:, :, 256 * kv:256 * kv + 256].rearrange("p j (h d) -> p j h d", h=KV)
                    ins = dve.tensor_tensor(y, x, tab, ALU.mult)
                ins.then_inc(fs_step, 1)
                dve.wait_ge(fs_step, 2 * w + 1)
                dve.tensor_reduce(fs[:, w, :], prod[:, :, :].rearrange("p j c -> p c j"), AX.X, ALU.add).then_inc(fs_step, 1)
            dve.wait_ge(cmp_ps, 1)
            dve.tensor_copy(W["kct"][:, :, 0:31], B[5][:, 0:64].rearrange("p (a n) -> p a n", a=2)[:, :, 0:31]).then_inc(cmp_done, 1)
            dve.tensor_copy(W["vc"][:, :], B[6][0:31, 0:256]).then_inc(cmp_done, 1)


def toeplitz(table, row, r, width):
    return table.ap()[row, P - 1:P - 1 + P * (r - 1)].rearrange("(p r) -> p r", r=r - 1)[:, 0:width]


def phase_nsa_prompt(R, W):
    nc, I = R.nc, R.i
    UNITS = [(gs, kind, par, i) for gs in range(2) for kind in range(3) for par in range(2) for i in range(4)]
    NU = len(UNITS)
    done = lambda n: n + 1 + NU
    with ExitStack() as ctx:
        kvn = R.sb("kvn", [P, 4, 1536], ctx=ctx)
        kT = R.sb("kT", [P, 2, 2, SEQ], ctx=ctx)
        gate = R.sb("gate", [P, 4, NH, 3], ctx=ctx)
        tab = [[R.sb(f"tab{a}{b}", [P, W_NSA], ctx=ctx) for b in range(2)] for a in range(2)]
        qn = [R.sb(f"qn{a}", [P, 4, 2, HD], ctx=ctx) for a in range(2)]
        qT = [R.sb(f"qT{a}", [P, SEQ], ctx=ctx) for a in range(2)]
        e = [R.sb(f"e{a}", [P, SEQ], ctx=ctx) for a in range(2)]
        eT = [R.sb(f"eT{a}", [P, SEQ], ctx=ctx) for a in range(2)]
        o = [R.sb(f"o{a}", [P, 4, 2, HD], ctx=ctx) for a in range(2)]
        mx = R.sb("mx", [P, 4], ctx=ctx)
        nm = R.sb("nm", [P, 4], ctx=ctx)
        den = R.sb("den", [P, 4], ctx=ctx)
        dmax = R.sb("dmax", [P, 4], ctx=ctx)
        coef = R.sb("coef", [P, 4], ctx=ctx)
        tick = R.sb("tick", [P, 1], ctx=ctx)
        s = {n: R.sem("np_" + n, ctx) for n in ("kv_in", "gate_in", "kT_ps", "kT_ready", "gate_ready", "t_in0", "t_in1", "qT_ps",
             "qT_ready", "scores", "biased", "nmax", "exps", "eT_ps", "eT_ready", "pv", "coef", "merged", "o_out0", "o_out1", "o_free0", "o_free1")}
        block = ctx.enter_context(nc.Block())
        ps_s, ps_t, ps_o, ps_q = R.banks[0:2], R.banks[2:4], R.banks[4:6], R.banks[6:8]
        unit_sems = [s[n] for n in ("scores", "biased", "nmax", "exps", "eT_ps", "eT_ready", "pv", "merged")]

        def keys(kind, i):
            return 31 if kind == 2 else P * (i + 1)

        @block.sync
        def _(eng):
            eng.dma_start(kvn[:, :, :], R.proj[0:SEQ, C_KV:C_KV + 1536].rearrange("(t p) c -> p t c", p=P)).then_inc(s["kv_in"], 16)
            eng.dma_start(gate[:, :, :, :], R.proj[0:SEQ, C_GATE:C_GATE + 72].rearrange("(t p) c -> p t c", p=P)).then_inc(s["gate_in"], 16)

            def loads(pr, it):
                for gs in range(2):
                    eng.wait_ge(s["biased"], done(NU * (3 * pr + it) - NU + 24 * gs + 23))
                    for par in range(2):
                        h = (2 * pr + par) * G + gs + 2 * it
                        eng.dma_start(tab[gs][par][:, :], W["tab_view"](h)).then_inc(s[f"t_in{gs}"], 16)
                        eng.dma_start(qn[gs][:, :, par, :], R.proj[0:SEQ, bass.ds(h * HD, HD)].rearrange("(t p) c -> p t c", p=P)).then_inc(s[f"t_in{gs}"], 16)
            for pr in range(2):
                with eng.Fori(0, 3) as it:
                    loads(pr, it)

        @block.tensor
        def _(pe):
            pe.sem_inc(s["qT_ps"], 2)
            pe.wait_ge(s["kv_in"], 16)
            for kind in range(2):
                for pr in range(2):
                    for t in range(4):
                        last = pe.transpose(R.banks[2 * kind + pr][:, t * P:(t + 1) * P],
                                            kvn[:, t, (2 + 2 * kind) * 256 + pr * P:(2 + 2 * kind) * 256 + pr * P + P], R.ident[:, :])
                    last.then_inc(s["kT_ps"], 1)
            pe.wait_ge(s["kT_ready"], 4)

            def body(pr, it):
                base = NU * (3 * pr + it)
                for gs in range(2):
                    pe.wait_ge(s[f"t_in{gs}"], 64 * (3 * pr + it) + 64)
                    pe.wait_ge(s["qT_ready"], 2 * (3 * pr + it) + gs)
                    for t in range(4):
                        last = pe.transpose(ps_q[gs][:, t * P:(t + 1) * P], qn[gs][:, t, :, :], R.ident[:, :])
                    last.then_inc(s["qT_ps"], 1)
                for step in range(NU + 2):
                    if step < NU:
                        gs, kind, par, i = UNITS[step]
                        if step % 24 == 0:
                            pe.wait_ge(s["qT_ready"], 2 * (3 * pr + it) + gs + 1)
                        pe.wait_ge(s["biased"], done(base + step - 2))
                        at = slice(64 * par, 64 * par + 64)
                        k = W["kct"][at, pr, 0:31] if kind == 2 else kT[at, kind, pr, 0:keys(kind, i)]
                        pe.matmul(ps_s[step % 2][:, 0:keys(kind, i)], qT[gs][at, i * P:(i + 1) * P], k,
                                  start=True, stop=True).then_inc(s["scores"], 1)
                    if 1 <= step <= NU:
                        u = step - 1
                        gs, kind, par, i = UNITS[u]
                        pe.wait_ge(s["exps"], done(base + u))
                        pe.wait_ge(s["eT_ready"], done(base + u - 2))
                        for kt in range((keys(kind, i) + P - 1) // P):
                            n = min(P, keys(kind, i))
                            last = pe.transpose(ps_t[u % 2][0:n, kt * P:(kt + 1) * P], e[u % 2][:, kt * P:kt * P + n], R.ident[:, :])
                        last.then_inc(s["eT_ps"], 1)
                    if step >= 2:
                        u = step - 2
                        gs, kind, par, i = UNITS[u]
                        pe.wait_ge(s["eT_ready"], done(base + u))
                        pe.wait_ge(s["merged"], done(base + u - 2))
                        nk = (keys(kind, i) + P - 1) // P
                        n = min(P, keys(kind, i))
                        kv = 2 * pr + par
                        for kt in range(nk):
                            v = W["vc"][:, kv * HD:(kv + 1) * HD] if kind == 2 else kvn[:, kt, (3 + 2 * kind) * 256 + kv * HD:(3 + 2 * kind) * 256 + (kv + 1) * HD]
                            last = pe.matmul(ps_o[u % 2][:, 0:HD], eT[u % 2][0:n, kt * P:(kt + 1) * P], v,
                                             start=(kt == 0), stop=(kt == nk - 1))
                        last.then_inc(s["pv"], 1)
            for pr in range(2):
                with pe.Fori(0, 3) as it:
                    body(pr, it)

        @block.scalar
        def _(act):
            for x in (s["exps"], s["eT_ready"]):
                act.sem_inc(x, NU)
            act.wait_ge(s["gate_in"], 16)
            act.activation(gate[:, :, :, :], gate[:, :, :, :], ACT.Sigmoid).then_inc(s["gate_ready"], 1)
            for n in range(4):
                act.wait_ge(s["kT_ps"], n + 1)
                act.activation(kT[:, n // 2, n % 2, :], R.banks[n][:, :], ACT.Copy).then_inc(s["kT_ready"], 1)

            def body(pr, it):
                base = NU * (3 * pr + it)
                for gs in range(2):
                    act.wait_ge(s["qT_ps"], 2 * (3 * pr + it) + gs + 3)
                    act.activation(qT[gs][:, :], ps_q[gs][:, :], ACT.Copy, scale=HD ** -0.5).then_inc(s["qT_ready"], 1)
                for step in range(NU + 1):
                    if step < NU:
                        gs, kind, par, i = UNITS[step]
                        n = keys(kind, i)
                        act.wait_ge(s["nmax"], done(base + step))
                        act.activation(e[step % 2][:, 0:n], e[step % 2][:, 0:n], ACT.Exp, bias=nm[:, step % 4:step % 4 + 1],
                                       accum_out=den[:, step % 4:step % 4 + 1]).then_inc(s["exps"], 1)
                    if step >= 1:
                        u = step - 1
                        gs, kind, par, i = UNITS[u]
                        n = min(P, keys(kind, i))
                        wd = P * ((keys(kind, i) + P - 1) // P)
                        act.wait_ge(s["eT_ps"], done(base + u))
                        act.wait_ge(s["pv"], done(base + u - 2))
                        act.activation(eT[u % 2][0:n, 0:wd], ps_t[u % 2][0:n, 0:wd], ACT.Copy).then_inc(s["eT_ready"], 1)
            for pr in range(2):
                with act.Fori(0, 3) as it:
                    body(pr, it)

        @block.vector
        def _(dve):
            for x in (s["scores"], s["eT_ps"], s["pv"]):
                dve.sem_inc(x, NU)
            for x in (s["biased"], s["nmax"], s["coef"], s["merged"]):
                dve.sem_inc(x, NU)
            dve.wait_ge(s["gate_ready"], 1)

            def body(pr, it):
                base = NU * (3 * pr + it)
                for gs in range(2):
                    dve.wait_ge(s[f"t_in{gs}"], 64 * (3 * pr + it) + 64)
                for step in range(NU + 3):
                    if step < NU:
                        dve.wait_ge(s["scores"], done(base + step))
                        dve.wait_ge(s["eT_ps"], done(base + step - 2))
                    if step >= 3:
                        v = step - 3
                        d = dmax[:, v % 4:v % 4 + 1]
                        dve.wait_ge(s["pv"], done(base + v))
                        dve.tensor_scalar(d, den[:, v % 4:v % 4 + 1], TINY, None, ALU.max).then_inc(s["coef"], 1)
                    else:
                        dve.memset(tick[:, :], 0.0)
                    if step < NU:
                        u = step
                        gs, kind, par, i = UNITS[u]
                        n = keys(kind, i)
                        c0 = 384 - P * i
                        bias = tab[gs][par][:, c0 + 31:c0 + 31 + 16 * 30 + 1:16] if kind == 2 else tab[gs][par][:, c0:c0 + n]
                        dve.tensor_tensor_reduce(out=e[u % 2][:, 0:n], in0=ps_s[u % 2][:, 0:n], in1=bias, scale=1.0, scalar=-1e29,
                                                 op0=ALU.add, op1=ALU.max, accum_out=mx[:, u % 4:u % 4 + 1]).then_inc(s["biased"], 1)
                        dve.wait_ge(s["biased"], done(base + u))
                        dve.tensor_scalar(nm[:, u % 4:u % 4 + 1], mx[:, u % 4:u % 4 + 1], -1.0, None, ALU.mult).then_inc(s["nmax"], 1)
                    if step >= 3:
                        gs, kind, par, i = UNITS[v]
                        if kind == 0 and par == 0 and i == 0:
                            dve.wait_ge(s[f"o_free{gs}"], 3 * pr + it + 1)
                        branch = (1, 2, 0)[kind]
                        gcol = gate[:, i, bass.ds((2 * pr + par) * G + gs + 2 * it, 1), branch:branch + 1].rearrange("p a b -> p (a b)")
                        c = coef[:, v % 4:v % 4 + 1]
                        dve.wait_ge(s["coef"], NU + 3 * (base + v) + 1)
                        dve.reciprocal(d, d).then_inc(s["coef"], 1)
                        dve.wait_ge(s["coef"], NU + 3 * (base + v) + 2)
                        dve.tensor_tensor(c, d, gcol, ALU.mult).then_inc(s["coef"], 1)
                        dve.wait_ge(s["coef"], NU + 3 * (base + v) + 3)
                        dst = o[gs][:, i, par, :]
                        if kind == 0:
                            dve.tensor_scalar(dst, ps_o[v % 2][:, 0:HD], c, None, ALU.mult).then_inc(s["merged"], 1)
                        else:
                            dve.scalar_tensor_tensor(dst, ps_o[v % 2][:, 0:HD], c, dst, ALU.mult, ALU.add).then_inc(s["merged"], 1)
            for pr in range(2):
                with dve.Fori(0, 3) as it:
                    body(pr, it)

        @block.gpsimd
        def _(eng):
            W["copies"](eng)

            def body(pr, it):
                base = NU * (3 * pr + it)
                for gs in range(2):
                    eng.wait_ge(s["merged"], done(base + 24 * gs + 23))
                    for par in range(2):
                        h = (2 * pr + par) * G + gs + 2 * it
                        eng.dma_start(R.mixd[0:SEQ, bass.ds(h * HD, HD)].rearrange("(t p) c -> p t c", p=P),
                                      o[gs][:, :, par, :]).then_inc(s[f"o_out{gs}"], 16)
                    eng.wait_ge(s[f"o_out{gs}"], 32 * (3 * pr + it) + 32)
                    eng.sem_inc(s[f"o_free{gs}"], 1)
            for gs in range(2):
                eng.sem_inc(s[f"o_free{gs}"], 1)
            for pr in range(2):
                with eng.Fori(0, 3) as it:
                    body(pr, it)


def copy_old_rows(R, eng, b):
    I, O = R.i, R.o

    def flat(x, r0, r1, a):
        return x[0, bass.ds(b, 1), r0:r1].rearrange("b r k h d -> (b r k h d)").rearrange("(a c) -> a c", a=a)

    eng.dma_start(flat(O[5], 0, 508, 16), flat(I["cache_nsa_win"], 4, 512, 16)).then_inc(R.copied, 16)
    for g, (win, a) in enumerate(((128, 16), (512, 32), (2048, 128))):
        eng.dma_start(flat(O[7 + 2 * g], 0, win - 4, a), flat(I[f"cache_dil{g}"], 4, win, a)).then_inc(R.copied, 16)


def copy_new_rows(R, eng):
    O = R.o

    def copy(dst, src):
        eng.dma_start(dst, src).then_inc(R.copied, 16)
        R.copies += 1

    f4 = "r k h d -> r (k h d)"
    R.copies += 4 * DB
    copy(O[2][0, 0].rearrange(f4), R.proj[0:SEQ, C_KV:C_KV + 1024])
    copy(O[3][0].rearrange("b r k h d -> (b r) (k h d)"), R.proj[SEQ:TOK, C_KV:C_KV + 1024])
    copy(O[4][0, 0].rearrange(f4), R.proj[0:SEQ, C_KV + 1024:C_KV + 1536])
    for b in range(DB):
        copy(O[5][0, b, 508:512].rearrange(f4), R.proj[SEQ + 4 * b:SEQ + 4 * b + 4, C_KV + 1024:C_KV + 1536])
    for g, (win, _) in enumerate(DIL):
        keep = min(win, SEQ)
        for kv, c0 in enumerate((C_DK, C_DV)):
            copy(O[6 + 2 * g][0, 0, :, kv].rearrange("r h d -> r (h d)"), R.proj[SEQ - keep:SEQ, c0 + g * 512:c0 + g * 512 + 512])
            for b in range(DB):
                copy(O[7 + 2 * g][0, b, win - 4:win, kv].rearrange("r h d -> r (h d)"),
                     R.proj[SEQ + 4 * b:SEQ + 4 * b + 4, c0 + g * 512:c0 + g * 512 + 512])


def phase_end(R):
    nc = R.nc
    with ExitStack() as ctx:
        block = ctx.enter_context(nc.Block())

        @block.gpsimd
        def _(eng):
            eng.wait_ge(R.copied, 16 * R.copies)


def phase_dil_prompt(R):
    nc, I = R.nc, R.i
    HEADS = [(g, h) for g in range(NG) for h in range(DH)]
    UNITS = [(b, i) for b in range(len(HEADS)) for i in range(4)]
    NU = len(UNITS)
    with ExitStack() as ctx:
        qkv = [[R.sb(f"dn{x}{a}", [P, 4, 512], ctx=ctx) for x in "qkv"] for a in range(2)]
        tab = R.sb("dtab", [P, NG * DH, W_DIL], ctx=ctx)
        rmask = R.sb("rmask", [P, P], ctx=ctx)
        qkT = [[R.sb(f"dT{x}{a}", [P, SEQ], ctx=ctx) for x in "qk"] for a in range(2)]
        e = [R.sb(f"de{a}", [P, 256], ctx=ctx) for a in range(2)]
        eT = [R.sb(f"deT{a}", [P, 256], ctx=ctx) for a in range(2)]
        o = [R.sb(f"do{a}", [P, 4, 130], ctx=ctx) for a in range(2)]
        nm = R.sb("dnm", [P, 4], ctx=ctx)
        rd = R.sb("drd", [P, 4], ctx=ctx)
        s = {n: R.sem("dp_" + n, ctx) for n in ("in0", "in1", "in2", "tab_in", "tab_ready", "T_ps", "T_ready", "scores", "biased",
             "nmax", "exps", "eT_ps", "eT_ready", "pv", "rden", "merged", "out0", "out1")}
        block = ctx.enter_context(nc.Block())
        ps_s, ps_t, ps_o, ps_q = R.banks[0:2], R.banks[2:4], R.banks[4:6], R.banks[6:8]

        def tiles(g, i):
            return [i - 1, i] if g == 0 and i else [i]

        loads = [3, 3, 12]

        @block.sync
        def _(eng):
            for g in range(NG):
                if g == 2:
                    eng.wait_ge(s["pv"], 16)
                for x, c0 in enumerate((C_DQ, C_DK, C_DV)):
                    rows = R.proj[0:SEQ, c0 + 512 * g:c0 + 512 * g + 512]
                    if g == 0:
                        eng.dma_start(qkv[g % 2][x][:, :, :], rows.rearrange("(i p) c -> p i c", p=P)).then_inc(s[f"in{g}"], 16)
                    elif g == 1:
                        eng.dma_start(qkv[g % 2][x][:, :, :], rows.rearrange("(p i) c -> p i c", i=4)).then_inc(s[f"in{g}"], 16)
                    else:
                        for rr in range(4):
                            eng.dma_start(qkv[g % 2][x][32 * rr:32 * rr + 32, :, :],
                                          rows.rearrange("(s i r) c -> r s i c", i=4, r=4)[rr]).then_inc(s[f"in{g}"], 16)

        @block.gpsimd
        def _(eng):
            for t in range(NG * DH):
                eng.dma_start(tab[:, t, :], toeplitz(R.tabd, t, R_DIL, W_DIL)).then_inc(s["tab_in"], 16)
            eng.dma_start(rmask[:, :], I["res_mask"]).then_inc(s["tab_in"], 16)
            n_out = [0, 0]
            for b, (g, h) in enumerate(HEADS):
                eng.wait_ge(s["merged"], 4 * b + 4)
                rows = R.od[g, :, h, :]
                if g == 0:
                    parts = [(rows.rearrange("(i p) c -> p i c", p=P), o[b % 2][:, :, :])]
                elif g == 1:
                    parts = [(rows.rearrange("(p i) c -> p i c", i=4), o[b % 2][:, :, :])]
                else:
                    parts = [(rows.rearrange("(s i r) c -> r s i c", i=4, r=4)[rr], o[b % 2][32 * rr:32 * rr + 32, :, :]) for rr in range(4)]
                for dst, src in parts:
                    eng.dma_start(dst, src).then_inc(s[f"out{b % 2}"], 16)
                    n_out[b % 2] += 16
            for a in range(2):
                eng.wait_ge(s[f"out{a}"], n_out[a])

        @block.tensor
        def _(pe):
            def head_transposes(b):
                g, h = HEADS[b]
                pe.wait_ge(s[f"in{g}"], 16 * loads[g])
                for x in range(2):
                    if b:
                        pe.wait_ge(s["T_ready"], 2 * b - 1 + x)
                    for t in range(4):
                        last = pe.transpose(ps_q[x][:, t * P:(t + 1) * P], qkv[g % 2][x][:, t, h * DHD:(h + 1) * DHD], R.ident[:, :])
                    last.then_inc(s["T_ps"], 1)
            head_transposes(0)
            for step in range(NU + 2):
                if step < NU:
                    b, i = UNITS[step]
                    if i == 0:
                        pe.wait_ge(s["T_ready"], 2 * b + 2)
                    ks = tiles(HEADS[b][0], i)
                    if step >= 2:
                        pe.wait_ge(s["biased"], step - 1)
                    pe.matmul(ps_s[step % 2][:, 0:P * len(ks)], qkT[b % 2][0][:, i * P:(i + 1) * P],
                              qkT[b % 2][1][:, ks[0] * P:(ks[-1] + 1) * P], start=True, stop=True).then_inc(s["scores"], 1)
                    if i == 1 and b + 1 < len(HEADS):
                        head_transposes(b + 1)
                if 1 <= step <= NU:
                    u = step - 1
                    b, i = UNITS[u]
                    pe.wait_ge(s["exps"], u + 1)
                    if u >= 2:
                        pe.wait_ge(s["eT_ready"], u - 1)
                    for k in range(len(tiles(HEADS[b][0], i))):
                        last = pe.transpose(ps_t[u % 2][:, k * P:(k + 1) * P], e[u % 2][:, k * P:(k + 1) * P], R.ident[:, :])
                    last.then_inc(s["eT_ps"], 1)
                if step >= 2:
                    u = step - 2
                    b, i = UNITS[u]
                    g, h = HEADS[b]
                    pe.wait_ge(s["eT_ready"], u + 1)
                    if u >= 2:
                        pe.wait_ge(s["merged"], u - 1)
                    ks = tiles(g, i)
                    for k, t in enumerate(ks):
                        last = pe.matmul(ps_o[u % 2][:, 0:DHD], eT[u % 2][:, k * P:(k + 1) * P], qkv[g % 2][2][:, t, h * DHD:(h + 1) * DHD],
                                         start=(k == 0), stop=(k == len(ks) - 1))
                    last.then_inc(s["pv"], 1)

        @block.scalar
        def _(act):
            def head_evac(b):
                for x in range(2):
                    act.wait_ge(s["T_ps"], 2 * b + x + 1)
                    if b >= 2:
                        act.wait_ge(s["scores"], 4 * (b - 1))
                    act.activation(qkT[b % 2][x][:, :], ps_q[x][:, :], ACT.Copy, scale=DHD ** -0.5 if x == 0 else 1.0).then_inc(s["T_ready"], 1)
            head_evac(0)
            for step in range(NU + 1):
                if step < NU:
                    b, i = UNITS[step]
                    n = P * len(tiles(HEADS[b][0], i))
                    act.wait_ge(s["nmax"], step + 1)
                    act.activation(e[step % 2][:, 0:n], e[step % 2][:, 0:n], ACT.Exp, bias=nm[:, step % 4:step % 4 + 1],
                                   accum_out=o[b % 2][:, i, 129:130]).then_inc(s["exps"], 1)
                    if i == 1 and b + 1 < len(HEADS):
                        head_evac(b + 1)
                if step >= 1:
                    u = step - 1
                    b, i = UNITS[u]
                    n = P * len(tiles(HEADS[b][0], i))
                    act.wait_ge(s["eT_ps"], u + 1)
                    if u >= 2:
                        act.wait_ge(s["pv"], u - 1)
                    act.activation(eT[u % 2][:, 0:n], ps_t[u % 2][:, 0:n], ACT.Copy).then_inc(s["eT_ready"], 1)

        @block.vector
        def _(dve):
            dve.wait_ge(s["tab_in"], 16 * (NG * DH + 1))
            own = tab[:, 2 * DH:3 * DH, P:2 * P]
            dve.tensor_tensor(own, own, rmask[:, :].unsqueeze(1).to_broadcast([P, DH, P]), ALU.add).then_inc(s["tab_ready"], 1)
            dve.wait_ge(s["tab_ready"], 1)
            outs = [0, 0]
            for step in range(NU + 3):
                if step < NU:
                    u = step
                    b, i = UNITS[u]
                    g, h = HEADS[b]
                    n = P * len(tiles(g, i))
                    if i == 0 and b >= 2:
                        outs[b % 2] += 16 * (4 if HEADS[b - 2][0] == 2 else 1)
                        dve.wait_ge(s[f"out{b % 2}"], outs[b % 2])
                    dve.wait_ge(s["scores"], u + 1)
                    if u >= 2:
                        dve.wait_ge(s["eT_ps"], u - 1)
                    m = o[b % 2][:, i, 128:129]
                    dve.tensor_tensor_reduce(out=e[u % 2][:, 0:n], in0=ps_s[u % 2][:, 0:n], in1=tab[:, g * DH + h, 2 * P - n:2 * P],
                                             scale=1.0, scalar=-1e29, op0=ALU.add, op1=ALU.max, accum_out=m).then_inc(s["biased"], 1)
                    dve.wait_ge(s["biased"], u + 1)
                    dve.tensor_scalar(nm[:, u % 4:u % 4 + 1], m, -1.0, None, ALU.mult).then_inc(s["nmax"], 1)
                if step >= 3:
                    v = step - 3
                    b, i = UNITS[v]
                    r = rd[:, v % 4:v % 4 + 1]
                    dve.wait_ge(s["pv"], v + 1)
                    dve.reciprocal(r, o[b % 2][:, i, 129:130]).then_inc(s["rden"], 1)
                    dve.wait_ge(s["rden"], v + 1)
                    dve.tensor_scalar(o[b % 2][:, i, 0:DHD], ps_o[v % 2][:, 0:DHD], r, None, ALU.mult).then_inc(s["merged"], 1)


def merge_weights(dve, m, lse, w, tot, ready, wait_act, chain):
    step = [0]

    def link(ins):
        step[0] += 1
        ins.then_inc(chain, 1)
        dve.wait_ge(chain, step[0])

    wait_act(1)
    link(dve.tensor_tensor(lse, lse, m, ALU.add))
    link(dve.tensor_tensor(tot, lse[:, 0], lse[:, 1], ALU.max))
    link(dve.tensor_tensor(tot, tot, lse[:, 2], ALU.max))
    for g in range(NG):
        ins = dve.tensor_tensor(w[:, g], lse[:, g], tot, ALU.subtract)
    ins.then_inc(ready, 1)
    wait_act(2)
    link(dve.tensor_tensor(tot, w[:, 0], w[:, 1], ALU.add))
    link(dve.tensor_tensor(tot, tot, w[:, 2], ALU.add))
    link(dve.reciprocal(tot, tot))
    for g in range(NG):
        ins = dve.tensor_tensor(w[:, g], w[:, g], tot, ALU.mult)
    link(ins)
    return step[0]


def phase_dil_merge(R):
    nc = R.nc
    with ExitStack() as ctx:
        oc = R.sb("oc", [P, NG, 16, 130], ctx=ctx)
        lse = R.sb("lse", [P, NG, 16], ctx=ctx)
        w = R.sb("w", [P, NG, 16], ctx=ctx)
        tot = R.sb("tot", [P, 16], ctx=ctx)
        acc = R.sb("acc", [P, 16, DHD], ctx=ctx)
        s = {n: R.sem("dm_" + n, ctx) for n in ("in", "act", "dve", "chain", "out")}
        block = ctx.enter_context(nc.Block())

        @block.sync
        def _(eng):
            for g in range(NG):
                eng.dma_start(oc[:, g, :, :].rearrange("p (i h) c -> p i (h c)", i=4),
                              R.od[g].rearrange("(i p) h c -> p i (h c)", p=P)).then_inc(s["in"], 16)
            eng.wait_ge(s["dve"], 2)
            eng.dma_start(R.mixd[0:SEQ, NH * HD:D].rearrange("(i p) c -> p i c", p=P),
                          acc[:, :, :].rearrange("p (i h) c -> p i (h c)", i=4)).then_inc(s["out"], 16)
            eng.wait_ge(s["out"], 16)

        @block.scalar
        def _(act):
            act.wait_ge(s["in"], 48)
            act.activation(lse[:, :, :], oc[:, :, :, 129], ACT.Ln).then_inc(s["act"], 1)
            act.wait_ge(s["dve"], 1)
            act.activation(w[:, :, :], w[:, :, :], ACT.Exp).then_inc(s["act"], 1)

        @block.vector
        def _(dve):
            n = merge_weights(dve, oc[:, :, :, 128], lse[:, :, :], w[:, :, :], tot[:, :], s["dve"],
                              lambda k: dve.wait_ge(s["act"], k), s["chain"])
            for g in range(NG):
                ins = dve.tensor_tensor(oc[:, g, :, 0:DHD], oc[:, g, :, 0:DHD], w[:, g, :].unsqueeze(2).to_broadcast([P, 16, DHD]), ALU.mult)
            ins.then_inc(s["chain"], 1)
            dve.wait_ge(s["chain"], n + 1)
            dve.tensor_tensor(acc[:, :, :], oc[:, 0, :, 0:DHD], oc[:, 1, :, 0:DHD], ALU.add).then_inc(s["chain"], 1)
            dve.wait_ge(s["chain"], n + 2)
            dve.tensor_tensor(acc[:, :, :], acc[:, :, :], oc[:, 2, :, 0:DHD], ALU.add).then_inc(s["dve"], 1)


S_SEL, S_SNEW, S_WIN, S_WNEW, S_CMP = 0, PAST, PAST + NS, PAST + NS + 512, PAST + 2 * NS + 512
S_COLS = S_CMP + P
B_SEL, B_WIN, B_CMP, B_NEW = 0, PAST, PAST + 512, PAST + 512 + P
B_COLS = B_NEW + NS + 28


def phase_nsa_sample(R):
    nc, I = R.nc, R.i
    with ExitStack() as ctx:
        ring = R.ring[:, :, :, :].rearrange("p a b c -> p (a b c)")
        xt = R.xt[:, :, :].rearrange("p a b -> p (a b)")
        at = [0]

        def in_xt(n):
            at[0] += n
            assert at[0] <= KT * TOK
            return xt[:, at[0] - n:at[0]]

        odd_pages = R.sb("odd_pages", [P, 16, 1024], ctx=ctx)
        pages = [ring.rearrange("p (g c) -> p g c", g=16), odd_pages[:, :, :]]
        bias = R.sb("bias_s", [P, B_COLS], ctx=ctx)
        qbd_all = R.sb("qbd_all", [P, DB, 2, P], ctx=ctx)
        e = R.sb("e_s", [P, S_COLS], ctx=ctx)
        ws = R.sb("ws", [P, 8, 247], ctx=ctx)
        small = R.sb("small", [P, 512], ctx=ctx)
        kts = [in_xt(1024).rearrange("p (a c) -> p a c", a=2) for _ in range(2)]
        win = [in_xt(2048).rearrange("p (j c) -> p j c", j=4) for _ in range(2)]
        pts = [in_xt(512) for _ in range(2)]
        qbd = R.sb("qbd", [P, 2, P], ctx=ctx)
        kcn = R.sb("kcn", [P, 512], ctx=ctx)
        o_all = R.sb("o_all", [P, DB, HD], ctx=ctx)
        skv = in_xt(1536)[0:NS].rearrange("p (a b) -> p a b", a=6)
        gsum = R.sb("gsum", [P, P], ctx=ctx)
        knt = small[:, 0:128].rearrange("p (k a t) -> p k a t", k=2, a=2)
        gates = small[:, 128:152].rearrange("p (b c) -> p b c", c=3)
        overlap, forced = small[:, 152:185], small[:, 185:251]
        imp, imp2, m8 = small[:, 251:284], small[:, 284:317], small[:, 317:325]
        bmask = small[:, 325:358]
        idx_all = small[:, 358:486].bitcast(U32)
        rowid = small[:, 486:487]
        mxs, nms, dens, coefs = (small[:, 487 + 4 * k:491 + 4 * k] for k in range(4))
        neg1, mxn = small[:, 503:504], small[:, 504:506]
        spare = small[:, 506:507]
        idx = R.sb("idx", [P, 2, 16], U32, ctx=ctx)
        oh = ring[0:33, 0:4 * B_COLS].rearrange("p (q c) -> p q c", q=4)
        tail = 4 * B_COLS
        sq = ring[0:NS, tail:tail + 1536]
        tblq = ring[0:33, tail + 1536:tail + 2048].rearrange("p (q r) -> p q r", q=4)
        tbl = ring[0:33, tail + 2048:tail + 2084]
        oj = ring[0:32, tail + 2084:tail + 2084 + 9 * P]
        pool = ring[0:32, tail + 3240:tail + 3248]
        pt_i = ring[:, tail + 3248:tail + 3376].bitcast(I32)
        s = {n: R.sem("ns_" + n, ctx) for n in ("in", "kv_in", "gate_in", "tbl_in", "set", "ps", "setup", "setup_act", "idx_ready", "o_out",
             "idx_slot", "pg_free", "win_in0", "win_in1", "comp", "kc_ready", "qbd_ready", "kt_ps", "kt_ready", "s_ps", "s_read",
             "small_ps", "small_read", "nm", "exps", "pcn", "pt_ps", "pt_ready", "link", "fin")}
        pg_in = [[R.sem(f"pg_in{b}{c}", ctx) for c in range(4)] for b in range(2)]
        B = R.banks

        with nc.Block() as block:
            @block.sync
            def _(eng):
                for pr in range(2):
                    for par in range(2):
                        c0 = (2 * pr + par) * G * HD
                        eng.dma_start(sq.rearrange("p (r g a d) -> p r a g d", r=2, g=G, a=2)[:, pr, par],
                                      R.proj[SEQ:TOK, c0:c0 + G * HD].rearrange("t (g d) -> t g d", g=G)).then_inc(s["in"], 16)
                eng.dma_start(skv.rearrange("p a b -> p (a b)"), R.proj[SEQ:TOK, C_KV:C_KV + 1536]).then_inc(s["in"], 16)
                eng.dma_start(oh, I["oh_smp"].rearrange("p (q c) -> p q c", q=4)).then_inc(s["in"], 16)
                eng.dma_start(oj, I["oh_pool"]).then_inc(s["in"], 16)
                for kv in range(2):
                    eng.dma_start(pool[:, 4 * kv:4 * kv + 4], I["cmp_pool"][0, kv]).then_inc(s["in"], 16)
                eng.dma_start(gsum[:, :], I["group_sum"]).then_inc(s["in"], 16)
                eng.dma_start(overlap, I["overlap"]).then_inc(s["in"], 16)
                eng.dma_start(forced, I["forced"]).then_inc(s["in"], 16)
                eng.dma_start(rowid, I["rowid"]).then_inc(s["in"], 16)
                eng.dma_start(pt_i, I["page_table"].rearrange("b g -> (b g)").rearrange("(a c) -> a c", a=1).to_broadcast([P, P])).then_inc(s["in"], 16)
                eng.wait_ge(s["set"], 2)
                eng.dma_start(tbl[0:NBKT, :], I["rel_bias"]).then_inc(s["tbl_in"], 16)
                for h in range(NH):
                    r0 = 32 * (h // G) + 4 * (h % G)
                    eng.dma_start(gates[r0:r0 + 4, :, :], R.proj[SEQ:TOK, C_GATE + 3 * h:C_GATE + 3 * h + 3].rearrange("(b q) c -> q b c", q=DS)).then_inc(s["gate_in"], 16)

            @block.gpsimd
            def _(eng):
                eng.memset(tbl, NEG).then_inc(s["set"], 1)
                eng.memset(small[:, 128:152], 0.0).then_inc(s["set"], 1)
                eng.memset(tblq, 0.0).then_inc(s["set"], 1)
                eng.memset(qbd_all[:, :, :, :], 0.0).then_inc(s["set"], 1)
                eng.memset(ws[:, :, :], 0.0).then_inc(s["set"], 1)
                eng.memset(neg1, -1.0).then_inc(s["set"], 1)

            @block.scalar
            def _(act):
                act.wait_ge(s["gate_in"], 16 * NH)
                act.activation(gates, gates, ACT.Sigmoid).then_inc(s["setup_act"], 1)

            @block.tensor
            def _(pe):
                pe.wait_ge(s["in"], 16 * 14)
                for pr in range(2):
                    for g in range(G):
                        src = sq[:, (pr * G + g) * P:(pr * G + g + 1) * P]
                        last = pe.transpose(B[6][:, (pr * G + g) * NS:(pr * G + g + 1) * NS], src, R.ident[0:NS, 0:NS])
                last.then_inc(s["ps"], 1)
                for kind in range(2):
                    for pr in range(2):
                        last = pe.transpose(B[7][:, (2 * kind + pr) * NS:(2 * kind + pr + 1) * NS],
                                            skv[:, 2 + 2 * kind, pr * P:(pr + 1) * P], R.ident[0:NS, 0:NS])
                for m in range(9):
                    last = pe.matmul(B[7][:, P + 8 * m:P + 8 * m + 8], oj[:, m * P:(m + 1) * P], pool, start=True, stop=True)
                last.then_inc(s["ps"], 1)
                pe.wait_ge(s["setup"], 4)
                for q in range(DS):
                    for c in range(6):
                        w = min(512, B_COLS - 512 * c)
                        last = pe.matmul(B[c][:, 0:w], tblq[:, q, :], oh[:, q, 512 * c:512 * c + w], start=(q == 0), stop=(q == DS - 1))
                last.then_inc(s["ps"], 1)

            @block.vector
            def _(dve):
                dve.wait_ge(s["tbl_in"], 16)
                dve.wait_ge(s["set"], 6)
                for q in range(DS):
                    dst = tblq[:, q, :].rearrange("p (k r) -> p k r", k=KV)[:, :, 0:24].rearrange("p k (g q) -> p k g q", q=DS)[:, :, :, q]
                    dve.tensor_copy(dst, tbl[:, 0:NH].rearrange("p (k g) -> p k g", k=KV)).then_inc(s["setup"], 1)
                dve.wait_ge(s["in"], 16 * 14)
                dve.tensor_scalar(idx_all, pt_i, float(PAGE), rowid, ALU.mult, ALU.add).then_inc(s["setup"], 1)
                dve.wait_ge(s["ps"], 1)
                for pr in range(2):
                    for par in range(2):
                        rows = slice(64 * par, 64 * par + 64)
                        c0 = 32 * (2 * pr + par)
                        for g in range(G):
                            dve.tensor_scalar(qbd_all[rows, :, pr, c0 + 4 * g:c0 + 4 * g + 4],
                                              B[6][rows, (pr * G + g) * NS:(pr * G + g + 1) * NS].rearrange("p (b q) -> p b q", q=DS),
                                              HD ** -0.5, None, ALU.mult).then_inc(s["setup"], 1)
                dve.wait_ge(s["ps"], 2)
                dve.tensor_copy(small[:, 0:128], B[7][:, 0:128]).then_inc(s["setup"], 1)
                dve.tensor_copy(ws[:, :, 119:128], B[7][:, P:P + 72].rearrange("p (m k) -> p k m", k=8)).then_inc(s["setup"], 1)
                dve.wait_ge(s["ps"], 3)
                for c in range(6):
                    w = min(512, B_COLS - 512 * c)
                    dve.tensor_copy(bias[:, 512 * c:512 * c + w], B[c][:, 0:w]).then_inc(s["setup"], 1)

        CK = ("sel0", "cmp", "sel1", "sel2", "sel3", "win")
        CR = 64
        done = lambda n: n + 1 + CR
        b0, kt_b, s_b, sm, pt_b = B[0], B[1:3], B[3:5], B[5], B[6:8]
        width = lambda k: P - 1 if CK[k] == "cmp" else 512
        PT = [("cmp", S_CMP, P - 1), ("win", S_WIN, 512), ("winn", S_WNEW, NS)] + \
             [(f"sel{c}", 512 * c, 512) for c in range(4)] + [("seln", S_SNEW, NS)]

        with nc.Block() as block:
            @block.gpsimd
            def _(eng):
                def gather(it, bb):
                    nb = 2 * it + bb
                    eng.wait_ge(s["pg_free"], nb + CR)
                    eng.tensor_copy(idx[:, bb, :], idx_all[:, bass.ds(16 * nb, 16)]).then_inc(s["idx_slot"], 1)
                    eng.wait_ge(s["idx_slot"], nb + 1)
                    eng.tensor_tensor(spare[:, 0:1], neg1, neg1, ALU.add)
                    for g in range(N_PAGES):
                        eng.indirect_dma_start(out=pages[bb][:, g, :], out_offset=None, in_=I["cache_nsa"].rearrange("l n t a h d -> (l n t) (a h d)"),
                                               in_offset=bass.IndirectOffsetOnAxis(ap=idx[:, bb, g:g + 1], axis=0)).then_inc(pg_in[bb][g // 4], 16)
                eng.sem_inc(s["pg_free"], CR + 1)
                with eng.Fori(0, DB // 2) as it:
                    for bb in range(2):
                        gather(it, bb)
                eng.wait_ge(s["fin"], CR + DB)
                for h in range(NH):
                    r0 = 32 * (h // G) + 4 * (h % G)
                    eng.dma_start(R.mixd[SEQ:TOK, h * HD:(h + 1) * HD].rearrange("(b q) d -> q b d", q=DS), o_all[r0:r0 + 4, :, :]).then_inc(s["o_out"], 16)
                eng.wait_ge(s["o_out"], 16 * NH)

            @block.sync
            def _(eng):
                with eng.Fori(0, DB // 2) as it:
                    for bb in range(2):
                        nb = 2 * it + bb
                        eng.wait_ge(s["pg_free"], nb + CR)
                        eng.dma_start(win[bb].rearrange("p j c -> p (j c)"),
                                      I["cache_nsa_win"][0, bass.ds(nb, 1)].rearrange("b (p j) k h d -> p (b j k h d)", j=4)).then_inc(s[f"win_in{bb}"], 16)

            @block.tensor
            def _(pe):
                def compress(it, bb):
                    nb = 2 * it + bb
                    pe.wait_ge(s["kc_ready"], done(nb - 1))
                    for c in range(4):
                        pe.wait_ge(pg_in[bb][c], 64 * it + 64)
                        for g in range(4 * c, 4 * c + 4):
                            for k in range(8):
                                last = pe.matmul(b0[0:P - 1, 64 * k:64 * k + 64], ws[:, k, 120 - 8 * g:120 - 8 * g + P - 1],
                                                 pages[bb][:, g, 64 * k:64 * k + 64], start=(g == 0 and k == 0),
                                                 stop=(g == N_PAGES - 1), skip_group_check=True)
                    last.then_inc(s["comp"], 1)

                def transpose_keys(it, bb, k):
                    m = 6 * (2 * it + bb) + k
                    pe.wait_ge(s["kt_ready"], done(m - 1))
                    if CK[k] == "cmp":
                        pe.wait_ge(s["kc_ready"], done(2 * it + bb))
                    if CK[k] == "win":
                        pe.wait_ge(s[f"win_in{bb}"], 16 * it + 16)
                    for pr in range(2):
                        if CK[k] == "cmp":
                            last = pe.transpose(kt_b[pr][:, 0:P - 1], kcn[0:P - 1, pr * P:(pr + 1) * P], R.ident[0:P - 1, 0:P - 1])
                        for t in range(4 if CK[k] != "cmp" else 0):
                            src = win[bb][:, t, pr * P:(pr + 1) * P] if CK[k] == "win" else \
                                pages[bb][:, 4 * int(CK[k][3]) + t, 512 + pr * P:512 + (pr + 1) * P]
                            last = pe.transpose(kt_b[pr][:, t * P:(t + 1) * P], src, R.ident[:, :])
                    last.then_inc(s["kt_ps"], 1)

                def scores(it, bb, k):
                    m = 6 * (2 * it + bb) + k
                    pe.wait_ge(s["kt_ready"], done(m))
                    pe.wait_ge(s["s_read"], done(m - 2))
                    if k == 0:
                        pe.wait_ge(s["qbd_ready"], done(2 * it + bb))
                    for pr in range(2):
                        last = pe.matmul(s_b[k % 2][:, 0:width(k)], qbd[:, pr, :], kts[k % 2][:, pr, 0:width(k)], start=(pr == 0), stop=(pr == 1))
                    last.then_inc(s["s_ps"], 1)

                def new_scores(it, bb):
                    nb = 2 * it + bb
                    pe.wait_ge(s["small_read"], done(5 * nb + 1))
                    for kind in range(2):
                        for pr in range(2):
                            last = pe.matmul(sm[:, NS * kind:NS * kind + NS], qbd[:, pr, :], knt[:, kind, pr, :], start=(pr == 0), stop=(pr == 1))
                    last.then_inc(s["small_ps"], 1)

                def transpose_p(it, bb, x):
                    r = 8 * (2 * it + bb) + x
                    name, c0, n = PT[x]
                    which = 0 if name == "cmp" else 1 if name[:3] == "win" else 2
                    if name in ("win", "sel0"):
                        pe.wait_ge(s["exps"], done(3 * (2 * it + bb) + which))
                    if name == "cmp":
                        pe.wait_ge(s["pcn"], done(2 * it + bb))
                    pe.wait_ge(s["pt_ready"], done(r - 2))
                    for t in range((n + P - 1) // P):
                        w = min(P, n - t * P)
                        last = pe.transpose(pt_b[x % 2][0:w, t * P:(t + 1) * P], e[:, c0 + t * P:c0 + t * P + w], R.ident[:, :])
                    last.then_inc(s["pt_ps"], 1)

                def values(it, bb, x, first, end):
                    r = 8 * (2 * it + bb) + x
                    name, c0, n = PT[x]
                    if name not in ("winn", "seln"):
                        pe.wait_ge(s["pt_ready"], done(r + 1 if name in ("win", "sel3") else r))
                    for t in range((n + P - 1) // P):
                        w = min(P, n - t * P)
                        for kv in range(KV):
                            if name == "cmp":
                                v = kcn[0:P - 1, 256 + 64 * kv:320 + 64 * kv]
                            elif name == "win":
                                v = win[bb][:, t, 256 + 64 * kv:320 + 64 * kv]
                            elif name == "winn" or name == "seln":
                                v = skv[:, 5 if name == "winn" else 3, 64 * kv:64 * kv + 64]
                            else:
                                v = pages[bb][:, 4 * int(name[3]) + t, 768 + 64 * kv:832 + 64 * kv]
                            last = pe.matmul(sm[32 * kv:32 * kv + 32, 256:320], pts[x % 2][0:w, t * P + 32 * kv:t * P + 32 * kv + 32], v,
                                             start=(first and t == 0), stop=(end and (t + 1) * P >= n))
                    return last

                def before(it, bb):
                    nb = 2 * it + bb
                    transpose_keys(it, bb, 0)
                    transpose_keys(it, bb, 1)
                    scores(it, bb, 0)
                    scores(it, bb, 1)
                    transpose_keys(it, bb, 2)
                    transpose_p(it, bb, 0)
                    transpose_keys(it, bb, 3)
                    scores(it, bb, 2)
                    pe.wait_ge(s["pt_ready"], done(8 * nb))
                    pe.wait_ge(s["small_read"], done(5 * nb - 1))
                    pe.matmul(sm[:, 64:97], pts[0][0:P - 1, 0:P], overlap[0:P - 1, :], start=True, stop=True)
                    values(it, bb, 0, True, True).then_inc(s["small_ps"], 1)
                    transpose_keys(it, bb, 4)
                    scores(it, bb, 3)
                    pe.wait_ge(s["small_read"], done(5 * nb))
                    pe.matmul(sm[:, 128:161], gsum[:, :], imp, start=True, stop=True).then_inc(s["small_ps"], 1)
                    transpose_keys(it, bb, 5)
                    scores(it, bb, 4)
                    new_scores(it, bb)
                    scores(it, bb, 5)
                    transpose_p(it, bb, 1)
                    transpose_p(it, bb, 2)
                    pe.wait_ge(s["small_read"], done(5 * nb + 2))
                    values(it, bb, 1, True, False)
                    values(it, bb, 2, False, True).then_inc(s["small_ps"], 1)

                def after(it, bb):
                    nb = 2 * it + bb
                    transpose_p(it, bb, 3)
                    for x in range(3, 8):
                        if x < 7:
                            transpose_p(it, bb, x + 1)
                        if x == 3:
                            pe.wait_ge(s["small_read"], done(5 * nb + 3))
                        last = values(it, bb, x, x == 3, x == 7)
                    last.then_inc(s["small_ps"], 1)

                for n in ("kc_ready", "kt_ready", "pt_ready", "exps", "qbd_ready"):
                    pe.sem_inc(s[n], CR)
                compress(0, 0)
                with pe.Fori(0, DB // 2 - 1) as it:
                    before(it, 0)
                    compress(it, 1)
                    after(it, 0)
                    before(it, 1)
                    compress(it + 1, 0)
                    after(it, 1)
                last_it = DB // 2 - 1
                before(last_it, 0)
                compress(last_it, 1)
                after(last_it, 0)
                before(last_it, 1)
                after(last_it, 1)

            @block.scalar
            def _(act):
                def keys_evac(it, bb, k):
                    m = 6 * (2 * it + bb) + k
                    act.wait_ge(s["kt_ps"], done(m))
                    act.wait_ge(s["s_ps"], done(m - 2))
                    for pr in range(2):
                        ins = act.activation(kts[k % 2][:, pr, 0:width(k)], kt_b[pr][:, 0:width(k)], ACT.Copy)
                    ins.then_inc(s["kt_ready"], 1)

                def exps(it, bb, which):
                    c0, n = ((S_CMP, P - 1), (S_WIN, 512 + NS), (S_SEL, PAST + NS))[which]
                    act.wait_ge(s["nm"], done(3 * (2 * it + bb) + which))
                    act.activation(e[:, c0:c0 + n], e[:, c0:c0 + n], ACT.Exp, bias=nms[:, which:which + 1],
                                   accum_out=dens[:, which:which + 1]).then_inc(s["exps"], 1)

                def p_evac(it, bb, x):
                    name, c0, n = PT[x]
                    w, c = min(n, P), P * ((n + P - 1) // P)
                    r = 8 * (2 * it + bb) + x
                    act.wait_ge(s["pt_ps"], done(r))
                    act.activation(pts[x % 2][0:w, 0:c], pt_b[x % 2][0:w, 0:c], ACT.Copy).then_inc(s["pt_ready"], 1)

                def kc_evac(it, bb):
                    act.wait_ge(s["comp"], done(2 * it + bb))
                    act.activation(kcn[0:P - 1, :], b0[0:P - 1, :], ACT.Copy).then_inc(s["kc_ready"], 1)

                def before(it, bb):
                    nb = 2 * it + bb
                    act.wait_ge(s["s_ps"], done(6 * nb - 1))
                    act.activation(qbd[:, :, :], qbd_all[:, bass.ds(nb, 1), :, :].rearrange("p b a r -> p (b a) r"), ACT.Copy).then_inc(s["qbd_ready"], 1)
                    keys_evac(it, bb, 0)
                    keys_evac(it, bb, 1)
                    exps(it, bb, 0)
                    keys_evac(it, bb, 2)
                    p_evac(it, bb, 0)
                    for k in (3, 4, 5):
                        keys_evac(it, bb, k)
                    exps(it, bb, 1)
                    p_evac(it, bb, 1)
                    p_evac(it, bb, 2)
                    exps(it, bb, 2)

                def after(it, bb):
                    for x in range(3, 8):
                        p_evac(it, bb, x)

                kc_evac(0, 0)
                with act.Fori(0, DB // 2 - 1) as it:
                    before(it, 0)
                    kc_evac(it, 1)
                    after(it, 0)
                    before(it, 1)
                    kc_evac(it + 1, 0)
                    after(it, 1)
                last_it = DB // 2 - 1
                before(last_it, 0)
                kc_evac(last_it, 1)
                after(last_it, 0)
                before(last_it, 1)
                after(last_it, 1)

            @block.vector
            def _(dve):
                def add_bias(it, bb, k):
                    m = 6 * (2 * it + bb) + k
                    e0, q0 = {"cmp": (S_CMP, B_CMP), "win": (S_WIN, B_WIN)}.get(CK[k], (0, 0))
                    if CK[k][:3] == "sel":
                        e0 = q0 = 512 * int(CK[k][3])
                    w = width(k)
                    dve.wait_ge(s["s_ps"], done(m))
                    if k == 0:
                        dve.wait_ge(s["pt_ps"], done(8 * (2 * it + bb) - 1))
                    dve.tensor_tensor(e[:, e0:e0 + w], s_b[k % 2][:, 0:w], bias[:, q0:q0 + w], ALU.add).then_inc(s["s_read"], 1)

                def coef(it, bb, which, branch):
                    nb = 2 * it + bb
                    c = coefs[:, which:which + 1]
                    dve.wait_ge(s["exps"], done(3 * nb + which))
                    dve.reciprocal(c, dens[:, which:which + 1])
                    dve.drain()
                    if branch is not None:
                        dve.tensor_tensor(c, c, gates[:, bass.ds(nb, 1), branch:branch + 1].rearrange("p a b -> p (a b)"), ALU.mult)
                        dve.drain()
                    return c

                def select():
                    dve.tensor_tensor(imp2, imp2, forced[:, 33:66], ALU.add)
                    dve.drain()
                    for _ in range(2):
                        dve.max(m8, imp2)
                        dve.drain()
                        dve.match_replace(imp2, m8, imp2, -1.0)
                        dve.drain()
                    dve.tensor_scalar(bmask, imp2, -1.0, NEG, ALU.not_equal, ALU.mult)
                    dve.drain()

                def before(it, bb):
                    nb = 2 * it + bb
                    add_bias(it, bb, 0)
                    add_bias(it, bb, 1)
                    dve.drain()
                    dve.tensor_reduce(nms[:, 0:1], e[:, S_CMP:S_CMP + P - 1], AX.X, ALU.max, negate=True).then_inc(s["nm"], 1)
                    c = coef(it, bb, 0, None)
                    dve.tensor_scalar(e[:, S_CMP:S_CMP + P - 1], e[:, S_CMP:S_CMP + P - 1], c, None, ALU.mult).then_inc(s["pcn"], 1)
                    add_bias(it, bb, 2)
                    dve.wait_ge(s["small_ps"], done(5 * nb))
                    dve.tensor_copy(imp, sm[:, 64:97])
                    ob = o_all[:, bass.ds(nb, 1), :].rearrange("p a d -> p (a d)")
                    dve.tensor_scalar(ob, sm[:, 256:320], gates[:, bass.ds(nb, 1), 0:1].rearrange("p a b -> p (a b)"), None, ALU.mult).then_inc(s["small_read"], 1)
                    add_bias(it, bb, 3)
                    dve.wait_ge(s["small_ps"], done(5 * nb + 1))
                    dve.tensor_tensor(imp2, sm[:, 128:161], forced[:, 0:33], ALU.mult).then_inc(s["small_read"], 1)
                    dve.drain()
                    select()
                    add_bias(it, bb, 4)
                    dve.wait_ge(s["small_ps"], done(5 * nb + 2))
                    nbias = bias[:, bass.ds(B_NEW + 28 - 4 * nb, NS)]
                    dve.tensor_tensor(e[:, S_SNEW:S_SNEW + NS], sm[:, 0:NS], nbias, ALU.add)
                    dve.tensor_tensor(e[:, S_WNEW:S_WNEW + NS], sm[:, NS:2 * NS], nbias, ALU.add).then_inc(s["small_read"], 1)
                    add_bias(it, bb, 5)
                    dve.drain()
                    dve.tensor_reduce(nms[:, 1:2], e[:, S_WIN:S_WIN + 512 + NS], AX.X, ALU.max, negate=True).then_inc(s["nm"], 1)
                    sel = e[:, 0:PAST].rearrange("p (n t) -> p n t", t=64)
                    dve.tensor_tensor(sel, sel, bmask[:, 0:32].unsqueeze(2).to_broadcast([P, 32, 64]), ALU.add)
                    dve.drain()
                    dve.tensor_reduce(nms[:, 2:3], e[:, 0:PAST + NS], AX.X, ALU.max, negate=True).then_inc(s["nm"], 1)
                    c = coef(it, bb, 1, 2)
                    dve.wait_ge(s["small_ps"], done(5 * nb + 3))
                    dve.scalar_tensor_tensor(ob, sm[:, 256:320], c, ob, ALU.mult, ALU.add).then_inc(s["small_read"], 1)

                def after(it, bb):
                    nb = 2 * it + bb
                    c = coef(it, bb, 2, 1)
                    dve.wait_ge(s["small_ps"], done(5 * nb + 4))
                    ob = o_all[:, bass.ds(nb, 1), :].rearrange("p a d -> p (a d)")
                    dve.scalar_tensor_tensor(ob, sm[:, 256:320], c, ob, ALU.mult, ALU.add).then_inc(s["small_read"], 1)
                    dve.wait_ge(s["small_read"], done(5 * nb + 4))
                    dve.sem_inc(s["pg_free"], 1)
                    dve.sem_inc(s["fin"], 1)

                for n in ("s_read", "small_read", "nm", "pcn", "s_ps", "small_ps", "kt_ps", "pt_ps", "comp", "fin"):
                    dve.sem_inc(s[n], CR)
                with dve.Fori(0, DB // 2) as it:
                    for bb in range(2):
                        before(it, bb)
                        after(it, bb)


def phase_dil_sample(R, w_o):
    nc, I = R.nc, R.i
    with ExitStack() as ctx:
        xt = R.xt[:, :, :].rearrange("p a b -> p (a b)")
        sd = xt[0:NS, 0:4608].rearrange("p (x g c) -> p x g c", x=3, g=NG)
        oh = xt[0:33, 4608:4608 + NG * DS * 160].rearrange("p (g q c) -> p g q c", g=NG, q=DS)
        tiles = [R.sb(f"kv_tiles{a}", [P, 9, 512], ctx=ctx) for a in range(2)]
        kT = [R.sb(f"kTd{a}", [P, 512], ctx=ctx) for a in range(2)]
        qT = R.sb("qTd", [P, NG, DH, NS], ctx=ctx)
        knT = R.sb("knTd", [P, NG, DH, NS], ctx=ctx)
        sT = R.sb("sTd", [P, NG, P], ctx=ctx)
        e = R.sb("ed", [P, NG, 160], ctx=ctx)
        pT = R.sb("pTd", [P, NG, P], ctx=ctx)
        pnT = R.sb("pnTd", [NS, NG, P], ctx=ctx)
        bias = R.sb("biasd", [P, NG, 160], ctx=ctx)
        bmask = R.sb("bmaskd", [P, NS], ctx=ctx)
        tbl = R.sb("tbld", [33, 36], ctx=ctx)
        tblq = R.sb("tbldq", [33, NG, DS, P], ctx=ctx)
        st = {n: R.sb("d_" + n, [P, NG], ctx=ctx) for n in ("m", "nm", "den", "lse", "w", "rd")}
        tot = R.sb("d_tot", [P, 1], ctx=ctx)
        acc = R.sb("d_acc", [P, P], ctx=ctx)
        s = {n: R.sem("ds_" + n, ctx) for n in ("in", "tbl_in", "set", "ps", "setup", "used", "in0", "in1", "ps0", "ps1", "ready0", "ready1",
             "mm", "s_done", "sT_ready", "S_ps", "nm", "exps", "ln", "wexp", "wd", "link", "P_ready", "P_ps", "PT_ready", "new_ps", "acc")}
        B = R.banks
        block = ctx.enter_context(nc.Block())
        bank_T, bank_S, bank_x, bank_o, bank_n = B[0:2], B[2], B[3], B[4:7], B[7]

        CR = 18

        def tile(j):
            return (0, None) if j == 0 else (1 + (j - 1) // 4, (j - 1) % 4)

        @block.sync
        def _(eng):
            for n in range(4):
                R.load_half(eng, n, w_o, (n % 2) * 8 * P, (n // 2) * BLK)
            def wait_slot(kv, it, bb):
                if kv == 0:
                    eng.wait_ge(s["mm"], 18 * it + 9 * bb + CR - 9)
                elif kv == 1:
                    eng.wait_ge(s["used"], 2 * it + bb + 1)

            for kv in range(2):
                if kv == 1:
                    eng.wait_ge(s["mm"], 9 * DB + CR)
                with eng.Fori(0, DB // 2) as it:
                    for bb in range(2):
                        nb = 2 * it + bb
                        wait_slot(kv, it, bb)
                        for g, (win, dil) in enumerate(DIL):
                            src = I[f"cache_dil{g}"][0, bass.ds(nb, 1), :, kv].rearrange("b r h d -> (b r) (h d)").rearrange("(m j) c -> m j c", j=dil)
                            t0, n = (0, 1) if g == 0 else (1 + 4 * (g - 1), 4)
                            eng.dma_start(tiles[bb][:, t0:t0 + n, :], src[:, 0:n, :]).then_inc(s[f"in{bb}"], 16)

        @block.gpsimd
        def _(eng):
            eng.memset(tbl[:, :], NEG).then_inc(s["set"], 1)
            eng.memset(tblq[:, :, :, :], 0.0).then_inc(s["set"], 1)
            for x, c0 in enumerate((C_DQ, C_DK, C_DV)):
                eng.dma_start(sd[:, x].rearrange("p g c -> p (g c)"), R.proj[SEQ:TOK, c0:c0 + 1536]).then_inc(s["in"], 16)
            eng.dma_start(oh, I["oh_ds"].rearrange("p (g q c) -> p g q c", g=NG, q=DS)).then_inc(s["in"], 16)
            eng.dma_start(bmask[:, :], I["batch_mask"]).then_inc(s["in"], 16)
            eng.wait_ge(s["set"], 2)
            eng.dma_start(tbl[0:NBKT, :], I["rel_bias"]).then_inc(s["tbl_in"], 16)

        def slot(it, bb, j):
            return (9 * bb + j) % 2, 9 * it + (9 * bb + j) // 2

        @block.tensor
        def _(pe):
            pe.wait_ge(s["in"], 80)
            for x in range(2):
                for g in range(NG):
                    for h in range(DH):
                        last = pe.transpose(B[x][:, (g * DH + h) * NS:(g * DH + h + 1) * NS], sd[:, x, g, h * DHD:(h + 1) * DHD], R.ident[0:NS, 0:NS])
            last.then_inc(s["ps"], 1)
            pe.wait_ge(s["setup"], NG * DS)
            for g in range(NG):
                for q in range(DS):
                    last = pe.matmul(B[3][:, 160 * g:160 * g + 160], tblq[:, g, q, :], oh[:, g, q, :], start=(q == 0), stop=(q == DS - 1))
            last.then_inc(s["ps"], 1)
            pe.wait_ge(s["setup"], NG * DS + 3)
            pe.sem_inc(s["used"], 2)
            pe.sem_inc(s["ready0"], 1)
            pe.sem_inc(s["ready1"], 1)

            def transpose_tile(it, bb, j):
                a, k = slot(it, bb, j)
                if j == 0:
                    pe.wait_ge(s[f"in{bb}"], 48 * it + 48)
                pe.wait_ge(s[f"ready{a}"], k + 1)
                for h in range(DH):
                    last = pe.transpose(bank_T[a][:, h * P:(h + 1) * P], tiles[bb][:, j, h * DHD:(h + 1) * DHD], R.ident[:, :])
                last.then_inc(s[f"ps{a}"], 1)

            def score_tile(it, bb, j):
                a, k = slot(it, bb, j)
                g, q = tile(j)
                nb = 2 * it + bb
                pe.wait_ge(s[f"ready{a}"], k + 2)
                for h in range(DH):
                    n, o = (4, 0) if q is None else (1, q)
                    last = pe.matmul(bank_S[:, bass.ds(g * P + h * NS + o + 4 * nb, n)], kT[a][:, h * P:(h + 1) * P],
                                     qT[:, g, h, bass.ds(4 * nb + o, n)], start=True, stop=True)
                last.then_inc(s["mm"], 1)

            with pe.Fori(0, DB // 2) as it:
                for bb in range(2):
                    transpose_tile(it, bb, 0)
                    for j in range(9):
                        if j < 8:
                            transpose_tile(it, bb, j + 1)
                        score_tile(it, bb, j)
            pe.wait_ge(s["sT_ready"], 1)
            for g in range(NG):
                pe.transpose(bank_x[:, g * P:(g + 1) * P], sT[:, g, :], R.ident[:, :])
            for g in range(NG):
                for h in range(DH):
                    last = pe.matmul(bank_n[32 * h:32 * h + 32, g * NS:(g + 1) * NS], qT[:, g, h, :], knT[:, g, h, :], start=True, stop=True)
            last.then_inc(s["S_ps"], 1)
            pe.wait_ge(s["P_ready"], 1)
            for g in range(NG):
                pe.transpose(bank_x[:, g * P:(g + 1) * P], e[:, g, 0:P], R.ident[:, :])
            for g in range(NG):
                last = pe.transpose(bank_n[0:NS, g * P:(g + 1) * P], e[:, g, P:160], R.ident[:, :])
            last.then_inc(s["P_ps"], 1)
            pe.wait_ge(s["PT_ready"], 2)
            for h in range(DH):
                for g in range(NG):
                    pe.matmul(bank_n[:, h * NS:(h + 1) * NS], sd[:, 2, g, h * DHD:(h + 1) * DHD], pnT[:, g, h * NS:(h + 1) * NS],
                              start=(g == 0), stop=(g == NG - 1))
            with pe.Fori(0, DB // 2) as it:
                for bb in range(2):
                    nb = 2 * it + bb
                    pe.wait_ge(s[f"in{bb}"], 48 * (it + DB // 2) + 48)
                    for j in range(9):
                        g, q = tile(j)
                        for h in range(DH):
                            n, o = (4, 0) if q is None else (1, q)
                            last = pe.matmul(bank_o[g][:, bass.ds(h * NS + o + 4 * nb, n)], tiles[bb][:, j, h * DHD:(h + 1) * DHD],
                                             pT[:, g, bass.ds(h * NS + 4 * nb + o, n)], start=True, stop=True)
                    last.then_inc(s["used"], 1)

        def evac(eng, a, copy):
            with eng.Fori(0, DB // 2) as it:
                for bb in range(2):
                    for j in range(9):
                        sl, k = slot(it, bb, j)
                        if sl == a:
                            eng.wait_ge(s[f"ps{a}"], k + 1)
                            eng.wait_ge(s["mm"], 18 * it + 9 * bb + j + CR - 1)
                            copy(kT[a][:, :], bank_T[a][:, :]).then_inc(s[f"ready{a}"], 1)

        @block.scalar
        def _(act):
            act.wait_ge(s["setup"], NG * DS + 3)
            act.sem_inc(s["mm"], CR)
            evac(act, 0, lambda o, i: act.activation(o, i, ACT.Copy))
            for g in range(NG):
                act.wait_ge(s["nm"], g + 1)
                act.activation(e[:, g, :], e[:, g, :], ACT.Exp, bias=st["nm"][:, g:g + 1], accum_out=st["den"][:, g:g + 1]).then_inc(s["exps"], 1)
            act.wait_ge(s["exps"], NG)
            act.activation(st["lse"][:, :], st["den"][:, :], ACT.Ln).then_inc(s["ln"], 1)
            act.wait_ge(s["wd"], 1)
            act.activation(st["w"][:, :], st["w"][:, :], ACT.Exp).then_inc(s["ln"], 1)

        @block.vector
        def _(dve):
            dve.wait_ge(s["tbl_in"], 16)
            for g in range(NG):
                for q in range(DS):
                    dst = tblq[:, g, q, :].rearrange("p (h b q) -> p h b q", h=DH, q=DS)[:, :, :, q]
                    src = tbl[:, NH + g * DH:NH + (g + 1) * DH].unsqueeze(2).to_broadcast([33, DH, DB])
                    dve.tensor_copy(dst, src).then_inc(s["setup"], 1)
            dve.wait_ge(s["ps"], 1)
            dve.tensor_scalar(qT[:, :, :, :].rearrange("p g h t -> p (g h t)"), B[0][:, 0:384], DHD ** -0.5, None, ALU.mult).then_inc(s["setup"], 1)
            dve.tensor_copy(knT[:, :, :, :].rearrange("p g h t -> p (g h t)"), B[1][:, 0:384]).then_inc(s["setup"], 1)
            dve.wait_ge(s["ps"], 2)
            dve.tensor_copy(bias[:, :, :].rearrange("p g c -> p (g c)"), B[3][:, 0:480]).then_inc(s["setup"], 1)
            dve.wait_ge(s["setup"], NG * DS + 3)
            nb = bias[:, :, P:160]
            dve.tensor_tensor(nb, nb, bmask[:, :].unsqueeze(1).to_broadcast([P, NG, NS]), ALU.add)
            evac(dve, 1, dve.tensor_copy)
            dve.wait_ge(s["mm"], 9 * DB + CR)
            dve.tensor_copy(sT[:, :, :].rearrange("p g r -> p (g r)"), bank_S[:, 0:384]).then_inc(s["sT_ready"], 1)
            dve.wait_ge(s["S_ps"], 1)
            dve.tensor_tensor(e[:, :, 0:P], bank_x[:, 0:384].rearrange("p (g c) -> p g c", g=NG), bias[:, :, 0:P], ALU.add)
            dve.tensor_tensor(e[:, :, P:160], bank_n[:, 0:96].rearrange("p (g c) -> p g c", g=NG), bias[:, :, P:160], ALU.add)
            dve.drain()
            dve.tensor_reduce(st["m"][:, :], e[:, :, :], AX.X, ALU.max)
            dve.drain()
            dve.tensor_scalar(st["nm"][:, :], st["m"][:, :], -1.0, None, ALU.mult).then_inc(s["nm"], NG)
            n = merge_weights(dve, st["m"][:, :].unsqueeze(2), st["lse"][:, :].unsqueeze(2), st["w"][:, :].unsqueeze(2), tot[:, :], s["wd"],
                              lambda k: dve.wait_ge(s["ln"], k), s["link"])
            dve.reciprocal(st["rd"][:, :], st["den"][:, :])
            dve.drain()
            dve.tensor_tensor(st["w"][:, :], st["w"][:, :], st["rd"][:, :], ALU.mult)
            dve.drain()
            for g in range(NG):
                ins = dve.tensor_scalar(e[:, g, :], e[:, g, :], st["w"][:, g:g + 1], None, ALU.mult)
            ins.then_inc(s["P_ready"], 1)
            dve.wait_ge(s["P_ps"], 1)
            dve.tensor_copy(pT[:, :, :].rearrange("p g r -> p (g r)"), bank_x[:, 0:384]).then_inc(s["PT_ready"], 1)
            dve.tensor_copy(pnT[:, :, :].rearrange("p g r -> p (g r)"), bank_n[0:NS, 0:384]).then_inc(s["PT_ready"], 1)
            dve.wait_ge(s["used"], 2 + DB)
            dve.tensor_copy(acc[:, :], bank_n[:, 0:P])
            for g in range(NG):
                dve.drain()
                dst = R.dilT[:, :, :].rearrange("p h t -> p (h t)") if g == NG - 1 else acc[:, :]
                ins = dve.tensor_tensor(dst, bank_o[g][:, 0:P], acc[:, :], ALU.add)
            ins.then_inc(s["acc"], 1)


def phase_mix_transpose(R):
    nc = R.nc
    with ExitStack() as ctx:
        mn = R.sb("mn", [P, NTT, D], ctx=ctx)
        m_in = [R.sem(f"m_in{t}", ctx) for t in range(NTT)]
        mT_ps, mT_done = R.sem("mT_ps", ctx), R.sem("mT_done", ctx)
        block = ctx.enter_context(nc.Block())
        cols = lambda t: 3 if t == NTT - 1 else 4

        @block.sync
        def _(eng):
            for t, (t0, n) in enumerate(TT):
                w = 4 * cols(t) * P
                eng.dma_start(mn[0:n, t, 0:w], R.mixd[t0:t0 + n, 0:w]).then_inc(m_in[t], 16)

        @block.tensor
        def _(pe):
            u = 0
            for t, (t0, n) in enumerate(TT):
                pe.wait_ge(m_in[t], 16)
                for j in range(cols(t)):
                    if u >= 8:
                        pe.wait_ge(mT_done, u - 7)
                    for k in range(4):
                        last = pe.transpose(R.banks[u % 8][:, k * n:(k + 1) * n], mn[0:n, t, (4 * j + k) * P:(4 * j + k + 1) * P], R.ident[0:n, 0:n])
                    last.then_inc(mT_ps, 1)
                    u += 1

        def evac(eng, which, copy):
            u = 0
            for t, (t0, n) in enumerate(TT):
                for j in range(cols(t)):
                    eng.wait_ge(mT_ps, u + 1)
                    copy(R.xt[:, 4 * j:4 * j + 4, t0:t0 + n], R.banks[u % 8][:, 0:4 * n].rearrange("p (k n) -> p k n", n=n)).then_inc(mT_done, 1)
                    u += 1

        @block.scalar
        def _(act):
            evac(act, 0, lambda o, i: act.activation(o, i, ACT.Copy))

        @block.vector
        def _(dve):
            dve.tensor_copy(R.xt[:, 4 * 3:KT, SEQ:TOK], R.dilT[:, :, :])


def phase_norm(R, name, a_dram, x_rows, gate_row, ln, store, modulate):
    nc, I = R.nc, R.i
    with ExitStack() as ctx:
        a = [R.sb(f"{name}_a{i}", [P, D], ctx=ctx) for i in range(2)]
        x = [R.sb(f"{name}_x{i}", [P, D], ctx=ctx) for i in range(2)]
        h = [R.sb(f"{name}_h{i}", [P, D], ctx=ctx) for i in range(2)]
        vec = {n: R.sb(f"{name}_{n}", [P, D], ctx=ctx) for n in ("g", "sc", "sh", "lng", "lnb")}
        stats = R.sb(name + "_stats", [P, 2, 4, 6], ctx=ctx)
        mv = R.sb(name + "_mv", [P, 2, 2], ctx=ctx)
        rstd = R.sb(name + "_rstd", [P, 2], ctx=ctx)
        eps = R.sb(name + "_eps", [P, 1], ctx=ctx)
        s = {n: R.sem(f"{name}_{n}", ctx) for n in ("in0", "in1", "vec", "vec2", "eps", "summed", "stats", "sqrt", "normed",
             "affine", "x_done", "out0", "out1", "h_done", "hT_ps", "hT_done")}
        block = ctx.enter_context(nc.Block())
        rows = {"g": gate_row, "sh": 1, "sc": 2}
        used = ("g", "sc", "sh") if modulate else ("g",)

        @block.sync
        def _(eng):
            def load(t):
                t0, n = TT[t]
                if t >= 2:
                    eng.wait_ge(s[f"out{t % 2}"], 16 * (t // 2))
                    if modulate:
                        eng.wait_ge(s["h_done"], t - 1)
                eng.dma_start(a[t % 2][0:n, :], a_dram[t0:t0 + n, :]).then_inc(s[f"in{t % 2}"], 16)
                eng.dma_start(x[t % 2][0:n, :], x_rows(t)).then_inc(s[f"in{t % 2}"], 16)
            load(0)
            for n in used:
                eng.dma_start(vec[n][:, :], R.modd[0:1, rows[n] * D:(rows[n] + 1) * D].to_broadcast([P, D])).then_inc(s["vec"], 16)
            for n, src in (("lng", I["ln_g"]), ("lnb", I["ln_b"])):
                eng.dma_start(vec[n][:, :], src[0, ln:ln + 1, :].to_broadcast([P, D])).then_inc(s["vec"], 16)
            load(1)
            for t in range(2, NTT):
                load(t)
            eng.wait_ge(s["h_done" if modulate else "summed"], NTT - 1)
            for n in used:
                for b in range(DB):
                    eng.dma_start(vec[n][DS * b:DS * b + DS, :],
                                  R.modd[1 + b:2 + b, rows[n] * D:(rows[n] + 1) * D].to_broadcast([DS, D])).then_inc(s["vec2"], 16)

        @block.vector
        def _(dve):
            dve.memset(eps[:, :], EPS).then_inc(s["eps"], 1)
            dve.wait_ge(s["vec"], 16 * (len(used) + 2))

            def modulated(t):
                i, n = t % 2, TT[t][1]
                dve.wait_ge(s["x_done"], t + 1)
                if t >= 2:
                    dve.wait_ge(s["hT_ps"], 4 * (t - 1))
                dve.scalar_tensor_tensor(h[i][0:n, :], vec["sc"][0:n, :], 1.0, x[i][0:n, :], ALU.add, ALU.mult)
                dve.drain()
                dve.tensor_tensor(h[i][0:n, :], h[i][0:n, :], vec["sh"][0:n, :], ALU.add).then_inc(s["h_done"], 1)

            for t, (t0, n) in enumerate(TT):
                i = t % 2
                dve.wait_ge(s[f"in{i}"], 32 * (t // 2 + 1))
                if t == NTT - 1:
                    if modulate:
                        modulated(t - 1)
                    dve.wait_ge(s["vec2"], 16 * DB * len(used))
                dve.scalar_tensor_tensor(a[i][0:n, :], vec["g"][0:n, :], 1.0, a[i][0:n, :], ALU.add, ALU.mult)
                dve.drain()
                dve.scalar_tensor_tensor(x[i][0:n, :], x[i][0:n, :], ALPHA, a[i][0:n, :], ALU.mult, ALU.add).then_inc(s["summed"], 1)
                dve.drain()
                for c in range(4):
                    dve.bn_stats(stats[0:n, i, c, :], x[i][0:n, c * 512:(c + 1) * 512])
                dve.drain()
                dve.bn_aggr(mv[0:n, i, :], stats[0:n, i, :, :].rearrange("p c s -> p (c s)")).then_inc(s["stats"], 1)
                dve.wait_ge(s["sqrt"], t + 1)
                dve.reciprocal(rstd[0:n, i:i + 1], rstd[0:n, i:i + 1])
                dve.drain()
                dve.tensor_scalar(x[i][0:n, :], x[i][0:n, :], mv[0:n, i, 0:1], rstd[0:n, i:i + 1], ALU.subtract, ALU.mult).then_inc(s["normed"], 1)
                if modulate and 1 <= t < NTT - 1:
                    modulated(t - 1)
            if modulate:
                modulated(NTT - 1)

        @block.gpsimd
        def _(eng):
            for t, (t0, n) in enumerate(TT):
                i = t % 2
                eng.wait_ge(s["normed"], t + 1)
                eng.tensor_tensor(x[i][0:n, :], x[i][0:n, :], vec["lng"][0:n, :], ALU.mult).then_inc(s["affine"], 1)
                eng.wait_ge(s["affine"], t + 1)
                eng.tensor_tensor(x[i][0:n, :], x[i][0:n, :], vec["lnb"][0:n, :], ALU.add).then_inc(s["x_done"], 1)
                eng.wait_ge(s["x_done"], t + 1)
                eng.dma_start(store(t), x[i][0:n, :]).then_inc(s[f"out{i}"], 16)
            eng.wait_ge(s["out0"], 16 * 3)
            eng.wait_ge(s["out1"], 16 * 2)

        def evac(act, t):
            t0, n = TT[t]
            for j in range(4):
                u = 4 * t + j
                act.wait_ge(s["hT_ps"], u + 1)
                act.activation(R.xt[:, 4 * j:4 * j + 4, t0:t0 + n], R.banks[u % 8][:, 0:4 * n].rearrange("p (k n) -> p k n", n=n),
                               ACT.Copy).then_inc(s["hT_done"], 1)

        @block.scalar
        def _(act):
            act.wait_ge(s["eps"], 1)
            for t, (t0, n) in enumerate(TT):
                act.wait_ge(s["stats"], t + 1)
                act.activation(rstd[0:n, t % 2:t % 2 + 1], mv[0:n, t % 2, 1:2], ACT.Sqrt, bias=eps[0:n, :]).then_inc(s["sqrt"], 1)
                if modulate and t:
                    evac(act, t - 1)
            if modulate:
                evac(act, NTT - 1)

        @block.tensor
        def _(pe):
            if not modulate:
                return
            for t, (t0, n) in enumerate(TT):
                pe.wait_ge(s["h_done"], t + 1)
                for j in range(4):
                    u = 4 * t + j
                    if u >= 8:
                        pe.wait_ge(s["hT_done"], u - 7)
                    for k in range(4):
                        last = pe.transpose(R.banks[u % 8][:, k * n:(k + 1) * n], h[t % 2][0:n, (4 * j + k) * P:(4 * j + k + 1) * P], R.ident[0:n, 0:n])
                    last.then_inc(s["hT_ps"], 1)


def phase_router(R):
    nc, I = R.nc, R.i
    BIG = 1e30
    with ExitStack() as ctx:
        wr = R.sb("wr", [P, KT, 20], ctx=ctx)
        lg = R.sb("lg", [P, NTT, 20], ctx=ctx)
        br = R.sb("br", [P, 20], ctx=ctx)
        first = R.sb("first_w", [P, 16], ctx=ctx)
        m1, m2, m3, pg = (R.sb(f"rt_m{i}", [P, NTT], ctx=ctx) for i in range(4))
        t4, oh4 = (R.sb(f"rt_4{i}", [P, NTT, 4], ctx=ctx) for i in range(2))
        t16, oh1, oh2, le = (R.sb(f"rt_16{i}", [P, NTT, 16], ctx=ctx) for i in range(4))
        gt = R.sb("gt", [NE, TOK], ctx=ctx)
        s = {n: R.sem("rt_" + n, ctx) for n in ("in", "zero", "ps", "to_exp", "exp", "gates", "gT_ps", "gT", "out")}
        block = ctx.enter_context(nc.Block())

        @block.sync
        def _(eng):
            eng.dma_start(wr[:, :, 0:4], I["w_router_group"][0].rearrange("(k p) c -> p k c", p=P)).then_inc(s["in"], 16)
            eng.dma_start(wr[:, :, 4:20], I["w_router_expert"][0].rearrange("(k p) c -> p k c", p=P)).then_inc(s["in"], 16)
            eng.dma_start(br[:, 0:4], I["b_router_group"].to_broadcast([P, 4])).then_inc(s["in"], 16)
            eng.dma_start(br[:, 4:20], I["b_router_expert"].to_broadcast([P, 16])).then_inc(s["in"], 16)
            eng.dma_start(first[:, :], I["first"]).then_inc(s["in"], 16)
            eng.wait_ge(s["gT"], 2)
            eng.dma_start(R.gated, gt[:, :]).then_inc(s["out"], 16)
            eng.wait_ge(s["out"], 16)

        @block.tensor
        def _(pe):
            pe.wait_ge(s["in"], 80)
            for t, (t0, n) in enumerate(TT):
                for k in range(KT):
                    last = pe.matmul(R.banks[t][0:n, 0:20], R.xt[:, k, t0:t0 + n], wr[:, k, :], start=(k == 0), stop=(k == KT - 1))
                last.then_inc(s["ps"], 1)
            pe.wait_ge(s["gates"], 1)
            for t, (t0, n) in enumerate(TT):
                b = R.banks[5] if t < 4 else R.banks[6]
                last = pe.transpose(b[0:NE, (t % 4) * P:(t % 4) * P + n], le[0:n, t, :], R.ident[0:n, 0:n])
            last.then_inc(s["gT_ps"], 1)

        @block.scalar
        def _(act):
            act.wait_ge(s["to_exp"], 1)
            act.activation(t4[:, :, :], t4[:, :, :], ACT.Exp).then_inc(s["exp"], 1)
            act.wait_ge(s["to_exp"], 2)
            act.activation(m3[:, :], m3[:, :], ACT.Exp).then_inc(s["exp"], 1)

        @block.vector
        def _(dve):
            def bc(x, n):
                return x[:, :].unsqueeze(2).to_broadcast([P, NTT, n])

            def weights(n):
                return first[:, 0:n].unsqueeze(1).to_broadcast([P, NTT, n])

            def pick(dst, tmp, src, top, n):
                dve.tensor_reduce(top[:, :], src, AX.X, ALU.max)
                dve.drain()
                dve.tensor_tensor(tmp, src, bc(top, n), ALU.is_equal)
                dve.drain()
                dve.tensor_tensor(tmp, tmp, weights(n), ALU.mult)
                dve.drain()
                dve.tensor_reduce(pg_tmp[:, :], tmp, AX.X, ALU.max)
                dve.drain()
                dve.tensor_tensor(dst, tmp, bc(pg_tmp, n), ALU.is_equal)
                dve.drain()

            pg_tmp = m2
            dve.memset(lg[:, :, :], 0.0)
            dve.wait_ge(s["in"], 80)
            dve.drain()
            for t, (t0, n) in enumerate(TT):
                dve.wait_ge(s["ps"], t + 1)
                dve.tensor_tensor(lg[0:n, t, :], R.banks[t][0:n, 0:20], br[0:n, :], ALU.add)
            dve.drain()
            pick(oh4[:, :, :], t4[:, :, :], lg[:, :, 0:4], m1, 4)
            dve.tensor_tensor(t4[:, :, :], lg[:, :, 0:4], bc(m1, 4), ALU.subtract).then_inc(s["to_exp"], 1)
            dve.wait_ge(s["exp"], 1)
            dve.tensor_reduce(pg[:, :], t4[:, :, :], AX.X, ALU.add)
            dve.tensor_scalar(oh4[:, :, :], oh4[:, :, :], BIG, BIG, ALU.mult, ALU.subtract)
            dve.drain()
            for g in range(4):
                dve.tensor_tensor(le[:, :, 4 * g:4 * g + 4], lg[:, :, 4 + 4 * g:8 + 4 * g],
                                  oh4[:, :, g:g + 1].to_broadcast([P, NTT, 4]), ALU.add)
            dve.drain()
            pick(oh1[:, :, :], t16[:, :, :], le[:, :, :], m1, 16)
            dve.scalar_tensor_tensor(le[:, :, :].rearrange("p t e -> p (t e)"), oh1[:, :, :].rearrange("p t e -> p (t e)"), -2 * BIG,
                                     le[:, :, :].rearrange("p t e -> p (t e)"), ALU.mult, ALU.add)
            dve.drain()
            pick(oh2[:, :, :], t16[:, :, :], le[:, :, :], m3, 16)
            dve.tensor_tensor(m3[:, :], m3[:, :], m1[:, :], ALU.subtract).then_inc(s["to_exp"], 1)
            dve.wait_ge(s["exp"], 2)
            dve.tensor_scalar(m1[:, :], m3[:, :], 1.0, None, ALU.add)
            dve.drain()
            dve.tensor_tensor(m1[:, :], m1[:, :], pg[:, :], ALU.mult)
            dve.drain()
            dve.reciprocal(m1[:, :], m1[:, :])
            dve.drain()
            dve.tensor_tensor(m3[:, :], m3[:, :], m1[:, :], ALU.mult)
            dve.tensor_tensor(oh1[:, :, :], oh1[:, :, :], bc(m1, 16), ALU.mult)
            dve.drain()
            dve.tensor_tensor(oh2[:, :, :], oh2[:, :, :], bc(m3, 16), ALU.mult)
            dve.drain()
            dve.tensor_tensor(le[:, :, :], oh1[:, :, :], oh2[:, :, :], ALU.add).then_inc(s["gates"], 1)
            dve.wait_ge(s["gT_ps"], 1)
            dve.tensor_copy(gt[:, 0:SEQ], R.banks[5][0:NE, :]).then_inc(s["gT"], 1)
            dve.tensor_copy(gt[:, SEQ:TOK], R.banks[6][0:NE, 0:NS]).then_inc(s["gT"], 1)


def phase_experts(R, w_gu, first, hid, next_loads):
    nc = R.nc
    HT = TOK // 2
    with ExitStack() as ctx:
        gb = [R.sb(f"gb{i}", [P, TOK], ctx=ctx) for i in range(2)]
        sg = [R.sb(f"sg{i}", [P, HT], ctx=ctx) for i in range(2)]
        s = {n: R.sem("ex_" + n, ctx) for n in ("gb0", "gb1", "ps", "silu", "up", "hid")}
        block = ctx.enter_context(nc.Block())
        CR = 8
        done = lambda n: n + 1 + CR
        POS = [(j, part, th) for j in range(2) for part in range(2) for th in range(2)]

        @block.sync
        def _(eng):
            with eng.Fori(1, NE // 2) as it:
                for s_ in range(4):
                    eng.wait_ge(R.ring_used, 4 * (first + it) + s_ - 3)
                    src = w_gu[bass.ds(2 * it + s_ // 2, 1), (s_ % 2) * 8 * P:(s_ % 2 + 1) * 8 * P, :].rearrange("e (t p) c -> p (e t) c", p=P)
                    eng.dma_start(R.ring[:, s_, :, :], src).then_inc(R.ring_full[s_], 16)
            next_loads(eng, 4 * (first + NE // 2) - 3)

        @block.gpsimd
        def _(eng):
            with eng.Fori(0, NE // 2) as it:
                for ee in range(2):
                    n = 2 * it + ee
                    eng.wait_ge(s["hid"], done(4 * (n - 2) + 3))
                    eng.dma_start(gb[ee][:, :], R.gated[bass.ds(n, 1), :].to_broadcast([P, TOK])).then_inc(s[f"gb{ee}"], 16)

        @block.tensor
        def _(pe):
            for x in ("silu", "up"):
                pe.sem_inc(s[x], CR)
            with pe.Fori(0, NE // 2) as it:
                for ee in range(2):
                    n = 2 * it + ee
                    for p, (j, part, th) in enumerate(POS):
                        pe.wait_ge(s["up" if part else "silu"], done(4 * (n - 1) + 2 * j + th))
                        for half in range(2):
                            if p == 0:
                                pe.wait_ge(R.ring_full[2 * ee + half], 16 * (first + it) + 16)
                            for k in range(8):
                                c0 = part * DE + j * P
                                mm = pe.matmul(R.banks[p][:, 0:HT], R.ring[:, 2 * ee + half, k, c0:c0 + P],
                                               R.xt[:, 8 * half + k, th * HT:(th + 1) * HT],
                                               start=(half == 0 and k == 0), stop=(half == 1 and k == 7))
                        mm.then_inc(s["ps"], 1)
                    pe.wait_ge(s["ps"], 8 * n + 8)
                    pe.sem_inc(R.ring_used, 2)

        @block.scalar
        def _(act):
            with act.Fori(0, NE // 2) as it:
                for ee in range(2):
                    n = 2 * it + ee
                    for p, (j, part, th) in enumerate(POS):
                        if part:
                            continue
                        act.wait_ge(s["ps"], 8 * n + p + 1)
                        act.wait_ge(s["up"], done(4 * n + 2 * j + th - 2))
                        act.activation(sg[th][:, :], R.banks[p][:, 0:HT], ACT.Silu).then_inc(s["silu"], 1)

        @block.vector
        def _(dve):
            dve.sem_inc(s["hid"], CR)
            with dve.Fori(0, NE // 2) as it:
                for ee in range(2):
                    n = 2 * it + ee
                    dve.wait_ge(s[f"gb{ee}"], 16 * it + 16)
                    for p, (j, part, th) in enumerate(POS):
                        if not part:
                            continue
                        dst = hid[:, bass.ds(2 * n + j, 1), th * HT:(th + 1) * HT].rearrange("p a n -> p (a n)")
                        dve.wait_ge(s["ps"], 8 * n + p + 1)
                        dve.wait_ge(s["silu"], done(4 * n + 2 * j + th))
                        dve.tensor_tensor(dst, sg[th][:, :], R.banks[p][:, 0:HT], ALU.mult).then_inc(s["up"], 1)
                        dve.drain()
                        dve.tensor_tensor(dst, dst, gb[ee][:, th * HT:(th + 1) * HT], ALU.mult).then_inc(s["hid"], 1)


def build(nc, ins, outs):
    R = Prog(nc, ins, outs)
    w_in, w_o, w_gu, w_dn = ins["w_in"][0], ins["w_o"][0], ins["w_gate_up"][0], ins["w_down"][0].rearrange("e f d -> (e f) d")
    ada_rounds = 6 * D // BLK // 2
    proj_at = ada_rounds
    wo_at = proj_at + NBLK // 2
    gu_at = wo_at + D // BLK // 2
    dn_at = gu_at + NE // 2

    def load_gu(eng, wait):
        for s in range(4):
            R.load_half(eng, s, w_gu[s // 2], (s % 2) * 8 * P, 0, wait=wait + s)

    def load_dn(eng, wait):
        for s in range(4):
            R.load_half(eng, s, w_dn, s * 8 * P, 0, wait=wait + s)

    def x_rows(t):
        return ins["x_prompt"][0, t * P:(t + 1) * P, :] if t < 4 else ins["x_sample"].rearrange("b q d -> (b q) d")

    def y_rows(t):
        return outs[0][0, t * P:(t + 1) * P, :] if t < 4 else outs[1].rearrange("b q d -> (b q) d")

    with R.ctx:
        with ExitStack() as c:
            rown = R.sb("rown", [NH, R_NSA], ctx=c)
            rowd = R.sb("rowd", [DH, NG, R_DIL], ctx=c)
            phase_bias_rows(R, rown, rowd)
            phase_ada(R, ins["w_ada"][0], w_in)
            phase_gemm(R, "proj", R.xt, KT, w_in, NBLK, LASTW, proj_at, R.proj, lambda eng, wait: None,
                       begin=lambda eng: spread_bias_rows(R, rown, rowd, eng), beside=lambda eng, it: copy_old_rows(R, eng, it))
        with ExitStack() as c:
            W = {"kct": R.sb("kct", [P, 2, 32], ctx=c), "vc": R.sb("vc", [31, 256], ctx=c),
                 "tab_view": lambda h: toeplitz(R.tabn, h, R_NSA, W_NSA), "copies": lambda eng: copy_new_rows(R, eng)}
            phase_compress_prompt(R, W)
            phase_nsa_prompt(R, W)
        phase_dil_prompt(R)
        phase_dil_merge(R)
        phase_nsa_sample(R)
        phase_dil_sample(R, w_o)
        phase_mix_transpose(R)
        phase_gemm(R, "wo", R.xt, KT, w_o, D // BLK, BLK, wo_at, R.ad, load_gu)
        phase_norm(R, "n1", R.ad, x_rows, 0, 0, lambda t: R.x1d[TT[t][0]:TT[t][0] + TT[t][1], :], True)
        phase_router(R)
        with ExitStack() as c:
            hid = R.sb("hid", [P, 2 * NE, TOK], ctx=c)
            phase_experts(R, w_gu, gu_at, hid, load_dn)
            phase_gemm(R, "down", hid, 2 * NE, w_dn, D // BLK, BLK, dn_at, R.yd, lambda eng, wait: None)
        phase_norm(R, "n2", R.yd, lambda t: R.x1d[TT[t][0]:TT[t][0] + TT[t][1], :], 3, 1, y_rows, False)
        phase_end(R)


_OUTS = [(1, 512, 2048), (8, 4, 2048), (1, 1, 512, 4, 4, 64), (1, 8, 4, 4, 4, 64), (1, 1, 512, 2, 4, 64),
         (1, 8, 512, 2, 4, 64), (1, 1, 128, 2, 4, 128), (1, 8, 128, 2, 4, 128), (1, 1, 512, 2, 4, 128),
         (1, 8, 512, 2, 4, 128), (1, 1, 512, 2, 4, 128), (1, 8, 2048, 2, 4, 128)]


def kernel(**inputs):
    import numpy as _np
    import concourse.bacc as _bacc
    from concourse import mybir as _mybir
    from concourse.bass_utils import run_bass_kernel_spmd as _run

    nc = _bacc.Bacc("TRN2", target_bir_lowering=False, num_devices=1)
    arrays, ins = {}, {}
    for name, a in {**inputs, **shape_tables()}.items():
        a = _np.ascontiguousarray(a)
        arrays[f"in_{name}"] = a
        ins[name] = nc.dram_tensor(f"in_{name}", a.shape, _mybir.dt.from_np(a.dtype), kind="ExternalInput").ap()
    outs = [nc.dram_tensor(f"out_{i}", s, F32, kind="ExternalOutput").ap() for i, s in enumerate(_OUTS)]
    build(nc, ins, outs)
    r = _run(nc, [arrays], core_ids=[0])
    return tuple(r.results[0][f"out_{i}"] for i in range(len(_OUTS)))
```
